# Optimizing a Trainium2 kernel written in Bass

```python
import math
import jax, jax.numpy as jnp
from jax import lax
import numpy as np

D_MODEL = 2048
BATCH = 1
SEQ = 256
DEPTH = 2

N_MIXERS = 2
N_META = 16
BLOCK = 128
WINDOW = 128
A_HEAD_DIM = 64
A_Q_HEADS = D_MODEL // A_HEAD_DIM
A_KV_HEADS = A_Q_HEADS // 8
A_GROUP = A_Q_HEADS // A_KV_HEADS
A_WIDTH = A_Q_HEADS * A_HEAD_DIM
A_KV_WIDTH = A_KV_HEADS * A_HEAD_DIM
A_IN = 2 * A_WIDTH + 2 * A_KV_WIDTH
B_HEAD_DIM = 128
B_HEADS = D_MODEL // B_HEAD_DIM
B_WIDTH = B_HEADS * B_HEAD_DIM
B_IN = 4 * B_WIDTH
B_PAD = BLOCK - N_META
N_BUCKETS = 32
MAX_DISTANCE = 128
N_A_LAYERS = (DEPTH + 1) // 2
N_B_LAYERS = DEPTH // 2
DEEPNORM_ALPHA = (2.0 * DEPTH) ** 0.25
DEEPNORM_BETA = (8.0 * DEPTH) ** -0.25
LN_EPS = 1e-5
NEG = -1e30

kernel_name = "hybrid_swa_sink_stickbreak_deepnorm"

def layer_norm(x, g, b):
    xf = x.astype(jnp.float32)
    mu = jnp.mean(xf, axis=-1, keepdims=True)
    var = jnp.mean(jnp.square(xf - mu), axis=-1, keepdims=True)
    y = (xf - mu) * lax.rsqrt(var + LN_EPS) * g.astype(jnp.float32) + b.astype(jnp.float32)
    return y.astype(x.dtype)

def t5_bucket(dist):
    max_exact = N_BUCKETS // 2
    d = jnp.maximum(dist, 0)
    df = jnp.maximum(d, 1).astype(jnp.float32)
    large = max_exact + (jnp.log(df / max_exact) / math.log(MAX_DISTANCE / max_exact)
                         * (N_BUCKETS - max_exact)).astype(jnp.int32)
    large = jnp.minimum(large, N_BUCKETS - 1)
    return jnp.where(d < max_exact, d, large)

def head_bias(rel_bias, dist):
    return rel_bias[t5_bucket(dist)].astype(jnp.float32)

def sliding_window_sink_attention(q, k, v, sinks, rel_bias):
    f32 = jnp.float32
    b, L = q.shape[0], q.shape[1]
    n_blk = (L - N_META) // BLOCK
    q = q.reshape(b, L, A_KV_HEADS, A_GROUP, A_HEAD_DIM).astype(f32) * (A_HEAD_DIM ** -0.5)
    k = k.reshape(b, L, A_KV_HEADS, A_HEAD_DIM).astype(f32)
    v = v.reshape(b, L, A_KV_HEADS, A_HEAD_DIM).astype(f32)
    qm, km, vm = q[:, :N_META], k[:, :N_META], v[:, :N_META]
    qb = q[:, N_META:].reshape(b, n_blk, BLOCK, A_KV_HEADS, A_GROUP, A_HEAD_DIM)
    kb = k[:, N_META:].reshape(b, n_blk, BLOCK, A_KV_HEADS, A_HEAD_DIM)
    vb = v[:, N_META:].reshape(b, n_blk, BLOCK, A_KV_HEADS, A_HEAD_DIM)
    pad = ((0, 0), (1, 0), (0, 0), (0, 0), (0, 0))
    kl = jnp.concatenate([jnp.pad(kb, pad)[:, :-1], kb], axis=2)
    vl = jnp.concatenate([jnp.pad(vb, pad)[:, :-1], vb], axis=2)

    i = jnp.arange(BLOCK)
    c = jnp.arange(2 * BLOCK)
    d_loc = i[:, None] + BLOCK - c[None, :]
    ok_loc = (d_loc >= 0) & (d_loc < WINDOW)
    no_prev = (jnp.arange(n_blk)[:, None, None] == 0) & (c[None, None, :] < BLOCK)
    ok_loc = ok_loc[None] & ~no_prev
    bias_loc = jnp.moveaxis(head_bias(rel_bias, d_loc), -1, 0).reshape(
        A_KV_HEADS, A_GROUP, BLOCK, 2 * BLOCK)
    s_loc = jnp.einsum('bnqhgd,bnshd->bnhgqs', qb, kl) + bias_loc
    s_loc = jnp.where(ok_loc[:, None, None], s_loc, NEG)

    qpos = N_META + jnp.arange(n_blk)[:, None] * BLOCK + i[None, :]
    d_meta = qpos[..., None] - jnp.arange(N_META)
    bias_meta = head_bias(rel_bias, d_meta).reshape(
        n_blk, BLOCK, N_META, A_KV_HEADS, A_GROUP).transpose(0, 3, 4, 1, 2)
    s_meta = jnp.einsum('bnqhgd,bshd->bnhgqs', qb, km) + bias_meta

    sink_logit = sinks.astype(f32).reshape(A_KV_HEADS, A_GROUP, 1, 1)
    sink = jnp.broadcast_to(sink_logit, s_meta.shape[:-1] + (1,))
    p = jax.nn.softmax(jnp.concatenate([s_meta, s_loc, sink], axis=-1), axis=-1)
    o = (jnp.einsum('bnhgqs,bshd->bnqhgd', p[..., :N_META], vm)
         + jnp.einsum('bnhgqs,bnshd->bnqhgd', p[..., N_META:N_META + 2 * BLOCK], vl))
    o = o.reshape(b, n_blk * BLOCK, A_WIDTH)

    d_mm = jnp.arange(N_META)[:, None] - jnp.arange(N_META)[None, :]
    bias_mm = jnp.moveaxis(head_bias(rel_bias, d_mm), -1, 0).reshape(
        A_KV_HEADS, A_GROUP, N_META, N_META)
    s_mm = jnp.einsum('bqhgd,bshd->bhgqs', qm, km) + bias_mm
    s_mm = jnp.where(d_mm >= 0, s_mm, NEG)
    sink_m = jnp.broadcast_to(sink_logit, s_mm.shape[:-1] + (1,))
    p_mm = jax.nn.softmax(jnp.concatenate([s_mm, sink_m], axis=-1), axis=-1)
    o_m = jnp.einsum('bhgqs,bshd->bqhgd', p_mm[..., :N_META], vm).reshape(b, N_META, A_WIDTH)
    return jnp.concatenate([o_m, o], axis=1)

def stick_breaking_attention(q, k, v):
    f32 = jnp.float32
    b, L = q.shape[0], q.shape[1]
    n_blk = (L - N_META) // BLOCK
    q = q.reshape(b, L, B_HEADS, B_HEAD_DIM).astype(f32) * (B_HEAD_DIM ** -0.5)
    k = k.reshape(b, L, B_HEADS, B_HEAD_DIM).astype(f32)
    v = v.reshape(b, L, B_HEADS, B_HEAD_DIM).astype(f32)
    kpad = ((0, 0), (B_PAD, 0), (0, 0), (0, 0))
    kp = jnp.pad(k, kpad)
    vp = jnp.pad(v, kpad)
    kpos = jnp.arange((n_blk + 1) * BLOCK) - B_PAD
    upper = (jnp.arange(BLOCK)[:, None] >= jnp.arange(BLOCK)[None, :]).astype(f32)

    def block_out(qblk, qpos, n_kb):
        nq = qblk.shape[1]
        kk = kp[:, :n_kb * BLOCK]
        vv = vp[:, :n_kb * BLOCK]
        pos = kpos[:n_kb * BLOCK]
        z = jnp.einsum('bqhd,bshd->bhqs', qblk, kk)
        visible = (pos[None, :] >= 0) & (pos[None, :] < qpos[:, None])
        sp = jnp.where(visible, jax.nn.softplus(z), 0.0).reshape(b, B_HEADS, nq, n_kb, BLOCK)
        tw = jnp.einsum('bhqks,sj->bhqkj', sp, upper, precision=lax.Precision.HIGHEST)
        tot = tw[..., 0]
        later = lax.cumsum(tot, axis=3, reverse=True) - tot
        tail = (tw + later[..., None]).reshape(b, B_HEADS, nq, n_kb * BLOCK)
        w = jnp.exp(jnp.where(visible, z - tail, -jnp.inf))
        return jnp.einsum('bhqs,bshd->bqhd', w, vv)

    outs = [block_out(q[:, :N_META], jnp.arange(N_META), 1)]
    for n in range(n_blk):
        start = N_META + n * BLOCK
        qpos = start + jnp.arange(BLOCK)
        outs.append(block_out(q[:, start:start + BLOCK], qpos, n + 2))
    return jnp.concatenate(outs, axis=1).reshape(b, L, B_WIDTH)

def branch_a(h, w_in, sinks, w_out, rel_bias):
    z = h @ w_in
    q, k, v, gate = jnp.split(
        z, [A_WIDTH, A_WIDTH + A_KV_WIDTH, A_WIDTH + 2 * A_KV_WIDTH], axis=-1)
    o = sliding_window_sink_attention(q, k, v, sinks, rel_bias).astype(h.dtype)
    return (o * jax.nn.silu(gate)) @ w_out

def branch_b(h, w_in, w_out):
    z = h @ w_in
    q, k, v, gate = jnp.split(z, [B_WIDTH, 2 * B_WIDTH, 3 * B_WIDTH], axis=-1)
    o = stick_breaking_attention(q, k, v).astype(h.dtype)
    return (o * jax.nn.silu(gate)) @ w_out

def setup_inputs(seed: int = 0) -> dict:
    key = jax.random.key(seed)
    ks = jax.random.split(key, 10)
    f32 = jnp.float32
    nrm = jax.random.normal
    x = nrm(ks[0], (BATCH, SEQ, D_MODEL), f32)
    meta_tokens = nrm(ks[1], (N_META, D_MODEL), f32)
    rel_bias = 0.5 * nrm(ks[2], (N_BUCKETS, A_Q_HEADS), f32)
    w_in_a = nrm(ks[3], (N_A_LAYERS, D_MODEL, A_IN), f32) * D_MODEL ** -0.5
    sinks_a = 0.5 * nrm(ks[4], (N_A_LAYERS, A_Q_HEADS), f32)
    w_out_a = nrm(ks[5], (N_A_LAYERS, A_WIDTH, D_MODEL), f32) * (A_WIDTH ** -0.5 * DEEPNORM_BETA)
    w_in_b = nrm(ks[6], (N_B_LAYERS, D_MODEL, B_IN), f32) * D_MODEL ** -0.5
    w_out_b = nrm(ks[7], (N_B_LAYERS, B_WIDTH, D_MODEL), f32) * (B_WIDTH ** -0.5 * DEEPNORM_BETA)
    ln_g = 1.0 + 0.02 * nrm(ks[8], (DEPTH, D_MODEL), f32)
    ln_b = 0.02 * nrm(ks[9], (DEPTH, D_MODEL), f32)
    return {"x": x, "meta_tokens": meta_tokens, "rel_bias": rel_bias,
            "w_in_a": w_in_a, "sinks_a": sinks_a, "w_out_a": w_out_a,
            "w_in_b": w_in_b, "w_out_b": w_out_b, "ln_g": ln_g, "ln_b": ln_b}

def reference(x, meta_tokens, rel_bias, w_in_a, sinks_a, w_out_a, w_in_b, w_out_b, ln_g, ln_b):
    b = x.shape[0]
    meta = jnp.broadcast_to(meta_tokens.astype(x.dtype)[None], (b, N_META, D_MODEL))
    h = jnp.concatenate([meta, x], axis=1)
    for i in range(DEPTH):
        j = i // N_MIXERS
        if i % N_MIXERS == 0:
            y = branch_a(h, w_in_a[j], sinks_a[j], w_out_a[j], rel_bias)
        else:
            y = branch_b(h, w_in_b[j], w_out_b[j])
        h = layer_norm(DEEPNORM_ALPHA * h + y, ln_g[i], ln_b[i])
    return h[:, N_META:]


_drawn_inputs = setup_inputs


def setup_inputs(seed=0):
    import zlib

    import numpy as np

    out = dict(_drawn_inputs(seed))
    spreads = {}
    factors = {'rel_bias': 3.276, 'sinks_a': 35.307}
    for name, (base, spread) in spreads.items():
        noise = np.random.default_rng([zlib.crc32(name.encode()), seed]).standard_normal(out[name].shape)
        drawn = base * np.exp(spread * noise) if base else spread * noise
        out[name] = __import__('jax').numpy.asarray(drawn.astype(out[name].dtype))
    for name, factor in factors.items():
        out[name] = (out[name] * factor).astype(out[name].dtype)
    return out
```

```python
import numpy as np
import concourse.bass as bass
from concourse import mybir
from contextlib import ExitStack

D = 2048
META = 16
SEQ = 256
T = META + SEQ
BLK = 128
KT = D // 128
HALF = KT // 2
CW = 256
ALPHA = (2.0 * 2) ** 0.25
EPS = 1e-5
NEG = -1e30
A_HD = 64
A_SCALE = A_HD ** -0.5
B_SCALE = 128 ** -0.5
N_BUCKETS = 32
LOC = 384
TAB = LOC + T
SW = 272 + 144 + 16

P_K, P_V, P_Q0 = 0, 1, 2
A_ITERS = 8
P_OUT_A = P_Q0 + 2 * A_ITERS
P_B = P_OUT_A + D // CW
B_ITERS = 8
P_OUT_B = P_B + 4 * B_ITERS
N_PAIRS = P_OUT_B + D // CW
N_CHUNKS = 2 * N_PAIRS
RAW_SLOTS = 2
SPLIT_SLOTS = 4
AHEAD = SPLIT_SLOTS


def trunk(nc, xT, chunks, rel_bias, sinks, onehot, tab_mask, consts, ln_cols, ln_rows, table, out):
    f32, f32r = mybir.dt.float32, mybir.dt.float32r
    ALU, ACT, AX = mybir.AluOpType, mybir.ActivationFunctionType, mybir.AxisListType

    with ExitStack() as ctx:
        def sb(name, shape, dt=f32):
            return ctx.enter_context(nc.sbuf_tensor(name, shape, dt))

        def sem(name):
            return ctx.enter_context(nc.semaphore(name))

        raw = sb("raw", [128, RAW_SLOTS, HALF, CW])
        w_hi = sb("w_hi", [128, SPLIT_SLOTS, HALF, CW], f32r)
        w_lo = sb("w_lo", [128, SPLIT_SLOTS, HALF, CW], f32r)
        h = sb("h", [128, KT, T])
        x_hi = sb("x_hi", [128, KT, T], f32r)
        x_lo = sb("x_lo", [128, KT, T], f32r)
        og_hi = sb("og_hi", [128, KT, T], f32r)
        og_lo = sb("og_lo", [128, KT, T], f32r)
        ident = sb("ident", [128, 128])
        ident_r = sb("ident_r", [128, 128], f32r)
        causal_r = sb("causal_r", [128, 128], f32r)
        neg_upper_r = sb("neg_upper_r", [128, 128], f32r)
        neg_ones_r = sb("neg_ones_r", [128, 128], f32r)
        neg_upper_m = sb("neg_upper_m", [META, META])
        mean_w = sb("mean_w", [128, 128])
        ln_gb = sb("ln_gb", [128, 2, KT])
        neg_sink = sb("neg_sink", [128, A_ITERS * 12])
        sp_hi = sb("sp_hi", [128, 2, 384], f32r)
        sp_lo = sb("sp_lo", [128, 2, 384], f32r)
        small = sb("small", [128, 7, 12])
        row_max, neg_max, sink_exp, row_sum, denom, rinv, sink_shift = (small[:, n, :] for n in range(7))
        bn_out = sb("bn_out", [128, 2, D // CW, 6])
        bn_mv = sb("bn_mv", [128, 2, 4])

        work = sb("work", [128, 8192])

        def carve(sizes):
            at, views = 0, {}
            for name, shape in sizes:
                n = int(np.prod(shape))
                v = work[:, at:at + n]
                if len(shape) == 2:
                    v = v.rearrange("p (a b) -> p a b", b=shape[1])
                if len(shape) == 3:
                    v = v.rearrange("p (a b c) -> p a b c", b=shape[1], c=shape[2])
                views[name] = v
                at += n
            assert at <= 8192, at
            return views

        a = carve([("q", (2, T)), ("gate", (2, T)), ("og", (T,)), ("kT", (2, T)), ("V", (2, 256)), ("VM", (256,)),
                   ("k_cur", (T,)), ("V_cur", (2, 128)), ("VM_cur", (128,)), ("bias", (4, SW)), ("t", (4, SW)),
                   ("ptx", (2, 384)), ("pty", (2, T))])
        setup = carve([("skip", (4000,)), ("onehot", (TAB,)), ("mask", (TAB,)), ("rel", (N_BUCKETS,)),
                       ("consts", (4, 128)), ("tab", (TAB,)), ("sink", (A_ITERS * 12,))])
        ln = carve([("skip", (3400,)), ("shift", (T,)), ("pair", (T,)), ("c_sum", (T,)), ("sq_sum", (T,)),
                    ("sq", (2, T)), ("mu", (T,)), ("mu2", (T,)), ("rstd", (T,)), ("var", (T,))])
        b = carve([("q", (2, SEQ)), ("kT", (2, T)), ("vT", (2, T)), ("V", (2, 256)), ("VM", (2, 128)),
                   ("w", (2, 384)), ("wM", (2, SEQ)), ("sp", (2, 384)), ("spM", (2, SEQ)),
                   ("gate", (2, SEQ)), ("og", (SEQ,))])
        f = carve([("r", (2, D)), ("gb", (2, D))])

        bank = [ctx.enter_context(nc.psum_tensor(f"bank{n}", [128, 512], f32)) for n in range(8)]
        acc = bank[0:2]
        scores = o_a = bank[2:4]
        ptx_bank, pty_bank = bank[4:6], bank[6:8]
        z_bank, zM_bank, o_b = bank[2:4], bank[4], bank[5:7]

        raw_loaded = [sem(f"raw_loaded{s}") for s in range(RAW_SLOTS)]
        hi_ready, lo_ready, half_used = sem("hi_ready"), sem("lo_ready"), sem("half_used")
        tile_full = [sem("tile_full0"), sem("tile_full1")]
        tile_free = [sem("tile_free0"), sem("tile_free1")]
        x_loaded, consts_loaded, setup_loaded, consts_ready = (sem("x_loaded"), sem("consts_loaded"),
                                                               sem("setup_loaded"), sem("consts_ready"))
        x_hi_ready, x_lo_ready = sem("x_hi_ready"), sem("x_lo_ready")
        tab_psum, tab_ready, tab_stored, bias_loaded = (sem("tab_psum"), sem("tab_ready"), sem("tab_stored"),
                                                        sem("bias_loaded"))
        sink_ready = sem("sink_ready")
        vt_ready, v_copied, k_staged, v_staged = sem("vt_ready"), sem("v_copied"), sem("k_staged"), sem("v_staged")
        scores_ready, scores_read, max_ready, shift_step = (sem("scores_ready"), sem("scores_read"),
                                                            sem("max_ready"), sem("shift_step"))
        probs_exp, norm_step, probs_ready = sem("probs_exp"), sem("norm_step"), sem("probs_ready")
        pt_ready, pt_copied, pv_done = sem("pt_ready"), sem("pt_copied"), sem("pv_done")
        gate_exp, o_read, og_hi_ready, og_lo_ready = (sem("gate_exp"), sem("o_read"), sem("og_hi_ready"),
                                                      sem("og_lo_ready"))
        pair_sum, mean_ready, shift_ready = sem("pair_sum"), sem("mean_ready"), sem("shift_ready")
        c_ready, c_summed, sq_ready, sq_summed = sem("c_ready"), sem("c_summed"), sem("sq_ready"), sem("sq_summed")
        ln_step, normed, affine_ready = sem("ln_step"), sem("normed"), sem("affine_ready")
        z_ready, sp_abs, sp_exp, sp_ln = sem("z_ready"), sem("sp_abs"), sem("sp_exp"), sem("sp_ln")
        sp_ready, sp_hi_ready, sp_lo_ready = sem("sp_ready"), sem("sp_hi_ready"), sem("sp_lo_ready")
        tail_ready, vtb_ready, vb_copied = sem("tail_ready"), sem("vtb_ready"), sem("vb_copied")
        gateb_exp = sem("gateb_exp")
        gate_den, gateb_den, rs_guess = sem("gate_den"), sem("gateb_den"), sem("rs_guess")
        ht_ready, r_ready, rows_loaded = sem("ht_ready"), sem("r_ready"), sem("rows_loaded")
        summed, fin_step, out_ready, stored = sem("summed"), sem("fin_step"), sem("out_ready"), sem("stored")

        PT_A, PV_A, O_A = 2 * 4 * A_ITERS, 4 * A_ITERS, 2 * A_ITERS

        block = ctx.enter_context(nc.Block())

        X_GROUP_A, X_GROUP_B = 4, 2
        X_A, X_B = KT // X_GROUP_A, KT // X_GROUP_B

        @block.sync
        def _(sp):
            def load(n, slot):
                sp.dma_start(raw[:, slot, :, :].rearrange("p t c -> p (t c)"), chunks[n]) \
                  .then_inc(raw_loaded[slot], 16)

            for n in range(RAW_SLOTS):
                load(n, n)
            with sp.Fori(1, N_CHUNKS // RAW_SLOTS) as r:
                for s in range(RAW_SLOTS):
                    sp.wait_ge(lo_ready, RAW_SLOTS * (r - 1) + s + 1)
                    load(RAW_SLOTS * r + s, s)
            for j in range(2):
                for c in range(2):
                    sp.wait_ge(out_ready, 2 * j + c + 1)
                    sp.dma_start(out[j * 128:(j + 1) * 128, c * 1024:(c + 1) * 1024],
                                 f["r"][:, j, c * 1024:(c + 1) * 1024]).then_inc(stored, 16)
            sp.wait_ge(stored, 64)

        @block.tensor
        def _(pe):
            mm = nc.tensor.matmul

            def project(P, m_hi, m_lo, cols, x_from=None, between=None, token_major=False):
                for half in range(2):
                    pe.wait_ge(lo_ready, 2 * P + half + 1)
                    slot = 2 * half_slot(P) + half
                    for u in range(2):
                        if half == 0 and not (isinstance(P, int) and P == 0):
                            pe.wait_ge(tile_free[u], P)
                        for k in range(HALF):
                            kt = half * HALF + k
                            if x_from and u == 0 and kt % x_from[1] == 0:
                                pe.wait_ge(x_lo_ready, x_from[0] + kt // x_from[1] + 1)
                            whi, wlo = w_hi[:, slot, k, :], w_lo[:, slot, k, :]
                            if token_major:
                                rows = slice(u * 128, u * 128 + 128)
                                o = acc[u][:, 0:CW]
                                terms = ((m_hi[:, kt, rows], whi), (m_lo[:, kt, rows], whi),
                                         (m_hi[:, kt, rows], wlo))
                            else:
                                wc = slice(u * 128, u * 128 + 128)
                                o = acc[u][:, 0:cols.stop - cols.start]
                                terms = ((whi[:, wc], m_hi[:, kt, cols]), (whi[:, wc], m_lo[:, kt, cols]),
                                         (wlo[:, wc], m_hi[:, kt, cols]))
                            for n, (l, r) in enumerate(terms):
                                last = mm(o, l, r, start=(kt == 0 and n == 0), stop=(kt == KT - 1 and n == 2))
                        if half == 0 and u == 1:
                            last.then_inc(half_used, 1)
                        if half == 1:
                            last.then_inc(tile_full[u], 1)
                    if half == 0 and between:
                        between()

            ALL, SEQ_COLS = slice(0, T), slice(META, T)

            pe.wait_ge(setup_loaded, 16 * 6)
            mm(pty_bank[0][0:32, 0:LOC], setup["rel"][0:32, :], setup["onehot"][0:32, 0:LOC],
               start=True, stop=True)
            mm(pty_bank[1][0:32, 0:T], setup["rel"][0:32, :], setup["onehot"][0:32, LOC:TAB],
               start=True, stop=True).then_inc(tab_psum, 1)

            project(P_K, x_hi, x_lo, ALL, x_from=(0, X_GROUP_A))
            project(P_V, x_hi, x_lo, ALL)
            pe.wait_ge(consts_loaded, 16 * 3)
            for u in range(2):
                pe.wait_ge(tile_free[u], P_V + 1)
                vT = a["q"][:, u, :]
                nc.tensor.transpose(ptx_bank[u][:, 0:128], vT[:, 16:144], ident[:])
                nc.tensor.transpose(ptx_bank[u][:, 128:256], vT[:, 144:272], ident[:])
                nc.tensor.transpose(ptx_bank[u][0:16, 256:384], vT[:, 0:16], ident[:]).then_inc(vt_ready, 1)
            project(P_Q0, x_hi, x_lo, ALL)

            def scores_of(i):
                for c in range(4):
                    u, base = c // 2, 64 * (c % 2)
                    if c == 0:
                        pe.wait_ge(k_staged, i + 1)
                    if c % 2 == 0:
                        pe.wait_ge(tile_free[u], P_Q0 + 2 * i + 1)
                    if c >= 2:
                        pe.wait_ge(scores_read, 2 * (4 * i + c - 1))
                    elif not (isinstance(i, int) and i == 0):
                        pe.wait_ge(o_read, 2 * (i - 1) + c + 1)
                    q, k, s = a["q"][base:base + 64, u, :], a["k_cur"][base:base + 64, :], scores[c % 2]
                    mm(s[:, 0:272], q[:, 0:128], k[:, 0:272], start=True, stop=True)
                    mm(s[:, 272:416], q[:, 128:256], k[:, 0:144], start=True, stop=True)
                    mm(s[0:16, 416:432], q[:, 256:272], k[:, 0:16], start=True, stop=True) \
                        .then_inc(scores_ready, 1)

            def attend_a(i):
                def turn(c):
                    g = 4 * i + c
                    x, y, t = ptx_bank[c % 2], pty_bank[c % 2], a["t"][:, c, :]
                    pe.wait_ge(probs_ready, 3 * (g + 1))
                    if not (isinstance(i, int) and i == 0) or c >= 2:
                        pe.wait_ge(pt_copied, 2 * (g - 1))
                    nc.tensor.transpose(y[0:16, 0:128], t[:, 0:16], ident[:])
                    nc.tensor.transpose(y[0:16, 128:256], t[:, 272:288], ident[:])
                    nc.tensor.transpose(y[0:16, 256:272], t[0:16, 416:432], ident[0:16, 0:16])
                    nc.tensor.transpose(x[:, 0:128], t[:, 16:144], ident[:])
                    nc.tensor.transpose(x[:, 128:256], t[:, 288:416], ident[:])
                    nc.tensor.transpose(x[:, 256:384], t[:, 144:272], ident[:]).then_inc(pt_ready, 1)

                def value(c):
                    g = 4 * i + c
                    u, base = c // 2, 64 * (c % 2)
                    if c == 0:
                        pe.wait_ge(v_staged, 2 * (i + 1))
                    pe.wait_ge(pt_copied, 2 * (g + 1))
                    x, y = a["ptx"][:, c % 2, :], a["pty"][0:16, c % 2, :]
                    o, cols = o_a[u][base:base + 64, 0:T], slice(base, base + 64)
                    mm(o, a["VM_cur"][0:16, cols], y, start=True, stop=False)
                    mm(o[:, 0:256], a["V_cur"][:, 0, cols], x[:, 0:256], start=False, stop=False)
                    mm(o[:, 0:128], a["V_cur"][:, 1, cols], x[:, 256:384], start=False, stop=True) \
                        .then_inc(pv_done, 1)

                turn(0)
                for c in range(4):
                    if c < 3:
                        turn(c + 1)
                    value(c)

            def body_a(i, last):
                project(P_Q0 + 1 + 2 * i, x_hi, x_lo, ALL)
                if not last:
                    project(P_Q0 + 2 + 2 * i, x_hi, x_lo, ALL)
                attend_a(i)
                if not last:
                    scores_of(i + 1)

            scores_of(0)
            body_a(0, False)
            with pe.Fori(1, A_ITERS - 1) as i:
                body_a(i, False)
            body_a(A_ITERS - 1, True)

            pe.wait_ge(og_lo_ready, KT)
            project(P_OUT_A, og_hi, og_lo, ALL)

            def shift_mean():
                pe.wait_ge(pair_sum, 1)
                mm(bank[2][:, 0:T], mean_w[:], ln["pair"], start=True, stop=True).then_inc(mean_ready, 1)

            project(P_OUT_A + 1, og_hi, og_lo, ALL, between=shift_mean)
            with pe.Fori(1, 4) as j:
                for p in range(2):
                    project(P_OUT_A + 2 * j + p, og_hi, og_lo, ALL)
            pe.wait_ge(c_summed, KT)
            pe.wait_ge(sq_summed, KT)
            mm(bank[2][:, 0:T], mean_w[:], ln["c_sum"], start=True, stop=True).then_inc(mean_ready, 1)
            mm(bank[3][:, 0:T], mean_w[:], ln["sq_sum"], start=True, stop=True).then_inc(mean_ready, 1)

            def scores_b(i):
                for u in range(2):
                    pe.wait_ge(tile_free[u], P_B + 4 * i + 2)
                    z, q, k = z_bank[u], b["q"][:, u, :], b["kT"][:, u, :]
                    if u == 0:
                        pe.wait_ge(pt_copied, PT_A + 3 * i)
                    mm(z[:, 0:256], k[:, 16:144], q, start=True, stop=False)
                    mm(z[:, 256:384], k[:, 144:272], q[:, 128:256], start=False, stop=False)
                    mm(z[:, 0:128], ident_r[:], causal_r[:], start=False, stop=False)
                    mm(z[:, 256:384], ident_r[:], causal_r[:], start=False, stop=True).then_inc(z_ready, 1)
                for u in range(2):
                    m = mm(zM_bank[0:16, u * SEQ:(u + 1) * SEQ], b["kT"][:, u, 0:16], b["q"][:, u, :],
                           start=(u == 0), stop=(u == 1))
                m.then_inc(z_ready, 1)

            def tails(i):
                add = dict(start=False, stop=True, skip_group_check=True)
                for u in range(2):
                    pe.wait_ge(sp_lo_ready, 2 * i + u + 1)
                    for s in (sp_hi[:, u, :], sp_lo[:, u, :]):
                        mm(z_bank[u][:, 256:384], neg_upper_r[:], s[:, 256:384], **add)
                        mm(z_bank[u][:, 0:256], neg_upper_r[:], s[:, 0:256], **add)
                        m = mm(z_bank[u][:, 128:256], neg_ones_r[:], s[:, 256:384], **add)
                    m.then_inc(tail_ready, 1)
                pe.wait_ge(sp_ready, 3 * (i + 1))
                for u in range(2):
                    zm = zM_bank[0:16, u * SEQ:(u + 1) * SEQ]
                    for s in (sp_hi[:, u, :], sp_lo[:, u, :]):
                        mm(zm, neg_ones_r[:, 0:16], s[:, 0:256], **add)
                        mm(zm[:, 128:256], neg_ones_r[:, 0:16], s[:, 256:384], **add)
                    m = mm(zm, neg_upper_m[:], b["spM"][0:16, u, :], **add)
                m.then_inc(tail_ready, 1)

            def turn_values(i):
                for u in range(2):
                    pe.wait_ge(tile_free[u], P_B + 4 * i + 3)
                    if u == 0:
                        pe.wait_ge(o_read, O_A + 2 * i)
                    v, o = b["vT"][:, u, :], o_b[u]
                    nc.tensor.transpose(o[:, 0:128], v[:, 16:144], ident[:])
                    nc.tensor.transpose(o[:, 128:256], v[:, 144:272], ident[:])
                    nc.tensor.transpose(o[0:16, 256:384], v[:, 0:16], ident[:]).then_inc(vtb_ready, 1)

            def attend_b(i):
                pe.wait_ge(pt_copied, PT_A + 3 * (i + 1))
                for u in range(2):
                    pe.wait_ge(vb_copied, 4 * i + 2 * u + 2)
                    o, w = o_b[u], b["w"][:, u, :]
                    mm(o[:, 0:256], b["VM"][0:16, u, :], b["wM"][0:16, u, :], start=True, stop=False)
                    mm(o[:, 0:256], b["V"][:, u, 0:128], w[:, 0:256], start=False, stop=False)
                    mm(o[:, 128:256], b["V"][:, u, 128:256], w[:, 256:384], start=False, stop=True) \
                        .then_inc(pv_done, 1)

            with pe.Fori(0, B_ITERS) as i:
                P = P_B + 4 * i
                project(P, x_hi, x_lo, SEQ_COLS, x_from=(X_A, X_GROUP_B))
                project(P + 1, x_hi, x_lo, ALL)
                project(P + 2, x_hi, x_lo, ALL, between=lambda: scores_b(i))

                def mid():
                    tails(i)
                    turn_values(i)

                project(P + 3, x_hi, x_lo, SEQ_COLS, between=mid)
                attend_b(i)

            pe.wait_ge(o_read, O_A + 2 * B_ITERS)
            for n in range(8):
                j, tg = n // 4, n % 4
                if n >= 4:
                    pe.wait_ge(r_ready, n - 3)
                for q in range(4):
                    m = nc.tensor.transpose(bank[4 + n % 4][:, q * 128:(q + 1) * 128],
                                            h[:, 4 * tg + q, META + 128 * j:META + 128 * (j + 1)], ident[:])
                m.then_inc(ht_ready, 1)
            pe.wait_ge(og_lo_ready, O_A + KT)
            with pe.Fori(0, 4) as j:
                for p in range(2):
                    project(P_OUT_B + 2 * j + p, og_hi, og_lo, None, token_major=True)

        def wait_slot_free(eng, P, half):
            if isinstance(P, int) and P < 2:
                return
            eng.wait_ge(half_used if half == 0 else tile_full[1], P - 1)

        @block.scalar
        def _(act):
            A = nc.scalar.activation

            act.dma_start(h[:, 0:8, :], xT[:, 0:8, :]).then_inc(x_loaded, 16)
            act.dma_start(setup["rel"][0:32, :], rel_bias).then_inc(setup_loaded, 16)
            act.dma_start(setup["onehot"][0:32, :], onehot).then_inc(setup_loaded, 16)
            act.dma_start(setup["mask"][0:32, :], tab_mask).then_inc(setup_loaded, 16)
            act.dma_start(setup["consts"], consts[:, 0:4, :]).then_inc(setup_loaded, 16)
            act.dma_start(setup["sink"], sinks.to_broadcast([128, A_ITERS * 12])).then_inc(setup_loaded, 16)
            act.dma_start(neg_upper_m[:], consts[0:META, 2, 0:META]).then_inc(setup_loaded, 16)
            act.dma_start(h[:, 8:16, :], xT[:, 8:16, :]).then_inc(x_loaded, 16)
            act.dma_start(ident[:], consts[:, 0, :]).then_inc(consts_loaded, 16)
            act.dma_start(mean_w[:], consts[:, 4, :]).then_inc(consts_loaded, 16)
            act.dma_start(ln_gb[:], ln_cols).then_inc(consts_loaded, 16)

            def split_hi(P, half):
                slot = 2 * half_slot(P) + half
                act.wait_ge(raw_loaded[half], 16 * (P + 1))
                wait_slot_free(act, P, half)
                A(w_hi[:, slot, :, :], raw[:, half, :, :], ACT.Copy).then_inc(hi_ready, 1)

            def evac(P, u, dst, cols, scale=1.0):
                act.wait_ge(tile_full[u], P + 1)
                A(dst, acc[u][:, cols], ACT.Copy, scale=scale).then_inc(tile_free[u], 1)

            def x_part(n):
                act.wait_ge(x_loaded, 32)
                cut = slice(n * X_GROUP_A, (n + 1) * X_GROUP_A)
                A(x_hi[:, cut, :], h[:, cut, :], ACT.Copy).then_inc(x_hi_ready, 1)

            def guess_rstd(y, v, ready, at, done):
                act.wait_ge(ready, at)
                A(y, v, ACT.Ln).then_inc(rs_guess, 1)
                act.wait_ge(rs_guess, done + 1)
                A(y, y, ACT.Exp, scale=-0.5).then_inc(rs_guess, 1)

            x_part(0)
            split_hi(0, 0)
            x_part(1)
            x_part(2)
            x_part(3)
            split_hi(0, 1)
            act.wait_ge(setup_loaded, 16 * 6)
            for n, dst in enumerate((ident_r, causal_r, neg_upper_r, neg_ones_r)):
                A(dst[:], setup["consts"][:, n, :], ACT.Copy).then_inc(consts_ready, 1)
            split_hi(1, 0)
            split_hi(1, 1)
            for u in range(2):
                evac(P_K, u, a["kT"][:, u, :], slice(0, T))
            split_hi(2, 0)
            split_hi(2, 1)
            for u in range(2):
                evac(P_V, u, a["q"][:, u, :], slice(0, T))
            for u in range(2):
                act.wait_ge(vt_ready, u + 1)
                A(a["V"][:, :, u * 128:(u + 1) * 128],
                  ptx_bank[u][:, 0:256].rearrange("p (a b) -> p a b", b=128), ACT.Copy).then_inc(v_copied, 1)
                A(a["VM"][0:16, u * 128:(u + 1) * 128], ptx_bank[u][0:16, 256:384], ACT.Copy).then_inc(v_copied, 1)
            split_hi(3, 0)
            split_hi(3, 1)
            for u in range(2):
                evac(P_Q0, u, backwards(a["q"][:, u, :]), slice(0, T), A_SCALE)
            split_hi(4, 0)
            split_hi(4, 1)

            def body_a(i, last):
                Pg = P_Q0 + 1 + 2 * i
                act.wait_ge(shift_step, 2 * (i + 1))
                for c in range(4):
                    for s, (lo, n, rows) in enumerate(((0, 272, 128), (272, 144, 128), (416, 16, 16))):
                        col = 4 * s + c
                        t = a["t"][0:rows, c, lo:lo + n]
                        A(t, t, ACT.Exp, bias=neg_max[0:rows, col:col + 1],
                          accum_out=row_sum[0:rows, col:col + 1]).then_inc(probs_exp, 1)
                A(sink_exp, sink_shift, ACT.Exp).then_inc(probs_exp, 1)
                for u in range(2):
                    act.wait_ge(tile_full[u], Pg + 1)
                    if not (isinstance(i, int) and i == 0):
                        act.wait_ge(o_read, 2 * i)
                    A(a["gate"][:, u, :], acc[u][:, 0:T], ACT.Exp, scale=-1.0).then_inc(gate_exp, 1)
                split_hi(Pg + 2, 0)
                split_hi(Pg + 2, 1)
                if not last:
                    split_hi(Pg + 3, 0)
                    for u in range(2):
                        evac(Pg + 1, u, backwards(a["q"][:, u, :]), slice(0, T), A_SCALE)
                for c in range(4):
                    g = 4 * i + c
                    act.wait_ge(pt_ready, g + 1)
                    if not (isinstance(i, int) and i == 0) or c >= 2:
                        act.wait_ge(pv_done, g - 1)
                    A(a["ptx"][:, c % 2, :], ptx_bank[c % 2][:, 0:384], ACT.Copy).then_inc(pt_copied, 1)
                    A(a["pty"][0:16, c % 2, :], pty_bank[c % 2][0:16, 0:T], ACT.Copy).then_inc(pt_copied, 1)
                for u in range(2):
                    act.wait_ge(o_read, 2 * i + u + 1)
                    A(og_hi[:, 2 * i + u, :], a["og"], ACT.Copy).then_inc(og_hi_ready, 1)
                if not last:
                    split_hi(Pg + 3, 1)

            body_a(0, False)
            with act.Fori(1, A_ITERS - 1) as i:
                body_a(i, False)
            body_a(A_ITERS - 1, True)

            def out_a(P, t):
                split_hi(P + 2, 0)
                split_hi(P + 2, 1)
                for u in range(2):
                    act.wait_ge(c_ready, t + u + 1)
                    if not (isinstance(t, int) and t == 0):
                        act.wait_ge(sq_summed, t + u - 1)
                    A(ln["sq"][:, u, :], h[:, t + u, :], ACT.Square).then_inc(sq_ready, 1)

            act.wait_ge(mean_ready, 1)
            A(ln["shift"], bank[2][:, 0:T], ACT.Copy, scale=float(D // CW)).then_inc(shift_ready, 1)
            out_a(P_OUT_A, 0)
            out_a(P_OUT_A + 1, 2)
            with act.Fori(1, 4) as j:
                for p in range(2):
                    out_a(P_OUT_A + 2 * j + p, 4 * j + 2 * p)
            guess_rstd(ln["rstd"], ln["var"], ln_step, 6, 0)
            with act.Fori(0, X_B) as n:
                act.wait_ge(normed, n + 1)
                for u in range(2):
                    t = 2 * n + u
                    A(h[:, t, :], h[:, t, :], ACT.Identity, scale=ln_gb_at(ln_gb, 0, t),
                      bias=ln_gb_at(ln_gb, 1, t)).then_inc(affine_ready, 1)
                act.wait_ge(affine_ready, 2 * n + 2)
                A(x_hi[:, bass.ds(2 * n, 2), :], h[:, bass.ds(2 * n, 2), :], ACT.Copy).then_inc(x_hi_ready, 1)

            with act.Fori(0, B_ITERS) as i:
                P = P_B + 4 * i
                split_hi(P + 2, 0)
                for u in range(2):
                    evac(P, u, b["q"][:, u, :], slice(0, SEQ), B_SCALE)
                split_hi(P + 2, 1)
                split_hi(P + 3, 0)
                for u in range(2):
                    evac(P + 1, u, b["kT"][:, u, :], slice(0, T))
                split_hi(P + 3, 1)
                split_hi(P + 4, 0)
                parts = [(z_bank[0][:, 0:384], b["w"][:, 0, :]), (z_bank[1][:, 0:384], b["w"][:, 1, :]),
                         (zM_bank[0:16, 0:2 * SEQ], b["wM"][0:16].rearrange("p a b -> p (a b)"))]
                act.wait_ge(pv_done, PV_A + 2 * i)
                for n, (z, w) in enumerate(parts):
                    act.wait_ge(z_ready, 3 * i + n + 1)
                    A(w, z, ACT.Abs).then_inc(sp_abs, 1)
                for n, (z, w) in enumerate(parts):
                    act.wait_ge(sp_abs, 3 * i + n + 1)
                    A(w, w, ACT.Exp, scale=-1.0).then_inc(sp_exp, 1)
                for n, (z, w) in enumerate(parts):
                    act.wait_ge(sp_exp, 3 * i + n + 1)
                    A(w, w, ACT.Ln, bias=1.0).then_inc(sp_ln, 1)
                for u in range(2):
                    act.wait_ge(sp_ready, 3 * i + u + 1)
                    A(sp_hi[:, u, :], b["sp"][:, u, :], ACT.Copy).then_inc(sp_hi_ready, 1)
                split_hi(P + 4, 1)
                split_hi(P + 5, 0)
                for n, (z, w) in enumerate(parts):
                    act.wait_ge(tail_ready, 3 * i + n + 1)
                    A(w, z, ACT.Exp).then_inc(pt_copied, 1)
                for u in range(2):
                    act.wait_ge(vtb_ready, 2 * i + u + 1)
                    A(b["V"][:, u, :], o_b[u][:, 0:256], ACT.Copy).then_inc(vb_copied, 1)
                    A(b["VM"][0:16, u, :], o_b[u][0:16, 256:384], ACT.Copy).then_inc(vb_copied, 1)
                for u in range(2):
                    act.wait_ge(tile_full[u], P + 3 + 1)
                    A(b["gate"][:, u, :], acc[u][:, 0:SEQ], ACT.Exp, scale=-1.0).then_inc(gateb_exp, 1)
                split_hi(P + 5, 1)
                for u in range(2):
                    act.wait_ge(o_read, O_A + 2 * i + u + 1)
                    A(og_hi[:, 2 * i + u, 0:SEQ], b["og"], ACT.Copy).then_inc(og_hi_ready, 1)

            act.wait_ge(og_lo_ready, O_A + KT)
            act.dma_start(f["gb"], ln_rows.to_broadcast([128, 2, D])).then_inc(rows_loaded, 16)
            for n in range(8):
                j, tg = n // 4, n % 4
                act.wait_ge(ht_ready, n + 1)
                A(f["r"][:, j, tg * 512:(tg + 1) * 512], bank[4 + n % 4][:], ACT.Copy, scale=ALPHA) \
                    .then_inc(r_ready, 1)
            with act.Fori(0, 3) as j:
                for p in range(2):
                    split_hi(P_OUT_B + 2 + 2 * j + p, 0)
                    split_hi(P_OUT_B + 2 + 2 * j + p, 1)
            guess_rstd(bn_mv[:, :, 2:3], bn_mv[:, :, 1:2], fin_step, 3, 2)

        @block.vector
        def _(dve):
            V = nc.vector

            def split_lo(P, half):
                slot = 2 * half_slot(P) + half
                dve.wait_ge(raw_loaded[half], 16 * (P + 1))
                dve.wait_ge(hi_ready, 2 * P + half + 1)
                V.tensor_tensor(w_lo[:, slot, :, :], raw[:, half, :, :], w_hi[:, slot, :, :].bitcast(f32),
                                ALU.subtract).then_inc(lo_ready, 1)

            def x_rest(n, cut, first):
                dve.wait_ge(x_hi_ready, first + n + 1)
                V.tensor_tensor(x_lo[:, cut, :], h[:, cut, :], x_hi[:, cut, :].bitcast(f32), ALU.subtract) \
                 .then_inc(x_lo_ready, 1)

            V.memset(small[:], 0.0).then_inc(sink_ready, 1)
            for n in range(4):
                x_rest(n, slice(4 * n, 4 * n + 4), 0)
                if n == 0:
                    split_lo(0, 0)
            split_lo(0, 1)
            dve.wait_ge(setup_loaded, 16 * 6)
            dve.wait_ge(tab_psum, 1)
            V.tensor_tensor(setup["tab"][0:32, 0:LOC], pty_bank[0][0:32, 0:LOC], setup["mask"][0:32, 0:LOC],
                            ALU.add).then_inc(tab_ready, 1)
            V.tensor_tensor(setup["tab"][0:32, LOC:TAB], pty_bank[1][0:32, 0:T], setup["mask"][0:32, LOC:TAB],
                            ALU.add).then_inc(tab_ready, 1)
            V.tensor_scalar(neg_sink[:], setup["sink"], -1.0, None, ALU.mult).then_inc(sink_ready, 1)
            for P in range(1, 5):
                split_lo(P, 0)
                split_lo(P, 1)
            dve.wait_ge(sink_ready, 2)
            dve.wait_ge(consts_ready, 4)

            def body_a(i, last):
                Pg = P_Q0 + 1 + 2 * i
                dve.wait_ge(bias_loaded, 80 * (i + 1))
                dve.wait_ge(pt_ready, 4 * i)
                for c in range(4):
                    g = 4 * i + c
                    dve.wait_ge(scores_ready, g + 1)
                    V.tensor_tensor(a["t"][:, c, 0:416], scores[c % 2][:, 0:416], a["bias"][:, c, 0:416],
                                    ALU.add).then_inc(scores_read, 1)
                    V.tensor_tensor(a["t"][0:16, c, 416:432], scores[c % 2][0:16, 416:432],
                                    a["bias"][0:16, c, 416:432], ALU.add).then_inc(scores_read, 1)
                dve.wait_ge(scores_read, 8 * (i + 1))
                for s, (lo, n, rows) in enumerate(((0, 272, 128), (272, 144, 128), (416, 16, 16))):
                    V.reduce_max(row_max[0:rows, 4 * s:4 * s + 4], a["t"][0:rows, :, lo:lo + n], axis=AX.X) \
                     .then_inc(max_ready, 1)
                dve.wait_ge(max_ready, 3 * (i + 1))
                sink = neg_sink[:, bass.ds(12 * i, 12)]
                V.scalar_tensor_tensor(neg_max, row_max, -1.0, sink, ALU.mult, ALU.min).then_inc(shift_step, 1)
                dve.wait_ge(shift_step, 2 * i + 1)
                V.tensor_tensor(sink_shift, neg_max, sink, ALU.subtract).then_inc(shift_step, 1)
                for u in range(2):
                    dve.wait_ge(gate_exp, 2 * i + u + 1)
                    V.tensor_scalar(a["gate"][:, u, :], a["gate"][:, u, :], 1.0, None, ALU.add) \
                     .then_inc(gate_den, 1)
                    dve.wait_ge(gate_den, 4 * i + 2 * u + 1)
                    V.reciprocal(a["gate"][:, u, :], a["gate"][:, u, :]).then_inc(gate_den, 1)
                    dve.wait_ge(gate_den, 4 * i + 2 * u + 2)
                    V.tensor_tensor(a["gate"][:, u, :], acc[u][:, 0:T], a["gate"][:, u, :], ALU.mult) \
                     .then_inc(tile_free[u], 1)
                dve.wait_ge(probs_exp, 13 * (i + 1))
                V.tensor_tensor(denom, row_sum, sink_exp, ALU.add).then_inc(norm_step, 1)
                dve.wait_ge(norm_step, 2 * i + 1)
                V.reciprocal(rinv, denom).then_inc(norm_step, 1)
                dve.wait_ge(norm_step, 2 * i + 2)
                for c in range(4):
                    for s, (lo, n, rows) in enumerate(((0, 272, 128), (272, 144, 128), (416, 16, 16))):
                        col = 4 * s + c
                        t = a["t"][0:rows, c, lo:lo + n]
                        V.tensor_scalar(t, t, rinv[0:rows, col:col + 1], None, ALU.mult).then_inc(probs_ready, 1)
                split_lo(Pg + 2, 0)
                split_lo(Pg + 2, 1)
                if not last:
                    split_lo(Pg + 3, 0)
                for u in range(2):
                    dve.wait_ge(pv_done, 4 * i + 2 * u + 2)
                    dve.wait_ge(tile_free[u], Pg + 1)
                    if u or not (isinstance(i, int) and i == 0):
                        dve.wait_ge(og_lo_ready, 2 * i + u)
                    V.tensor_tensor(a["og"], backwards(o_a[u][:, 0:T]), a["gate"][:, u, :], ALU.mult).then_inc(o_read, 1)
                    dve.wait_ge(o_read, 2 * i + u + 1)
                    dve.wait_ge(og_hi_ready, 2 * i + u + 1)
                    V.tensor_tensor(og_lo[:, 2 * i + u, :], a["og"], og_hi[:, 2 * i + u, :].bitcast(f32),
                                    ALU.subtract).then_inc(og_lo_ready, 1)
                if not last:
                    split_lo(Pg + 3, 1)

            body_a(0, False)
            with dve.Fori(1, A_ITERS - 1) as i:
                body_a(i, False)
            body_a(A_ITERS - 1, True)

            def residual(P, u, t):
                dve.wait_ge(tile_full[u], P + 1)
                V.scalar_tensor_tensor(h[:, t, :], h[:, t, :], ALPHA, acc[u][:, 0:T], ALU.mult, ALU.add) \
                 .then_inc(tile_free[u], 1)
                dve.wait_ge(tile_free[u], P + 1)

            def shifted(t):
                V.tensor_tensor(h[:, t, :], h[:, t, :], ln["shift"], ALU.subtract).then_inc(c_ready, 1)
                dve.wait_ge(c_ready, t + 1)
                V.tensor_tensor(ln["c_sum"], ln["c_sum"], h[:, t, :], ALU.add).then_inc(c_summed, 1)
                dve.wait_ge(c_summed, t + 1)

            def squared(t, u):
                dve.wait_ge(sq_ready, t + 1)
                V.tensor_tensor(ln["sq_sum"], ln["sq_sum"], ln["sq"][:, u, :], ALU.add).then_inc(sq_summed, 1)
                dve.wait_ge(sq_summed, t + 1)

            def out_a(P, t):
                for u in range(2):
                    residual(P, u, t + u)
                    shifted(t + u)
                split_lo(P + 2, 0)
                split_lo(P + 2, 1)
                for u in range(2):
                    squared(t + u, u)

            V.memset(ln["c_sum"], 0.0).then_inc(ln_step, 1)
            V.memset(ln["sq_sum"], 0.0).then_inc(ln_step, 1)
            dve.wait_ge(ln_step, 2)
            for u in range(2):
                residual(P_OUT_A, u, u)
            V.tensor_tensor(ln["pair"], h[:, 0, :], h[:, 1, :], ALU.add).then_inc(pair_sum, 1)
            dve.wait_ge(shift_ready, 1)
            for u in range(2):
                shifted(u)
            split_lo(P_OUT_A + 2, 0)
            split_lo(P_OUT_A + 2, 1)
            for u in range(2):
                squared(u, u)
            out_a(P_OUT_A + 1, 2)
            with dve.Fori(1, 4) as j:
                for p in range(2):
                    out_a(P_OUT_A + 2 * j + p, 4 * j + 2 * p)

            def rstd(y, v, tmp, step, at, guess_at):
                V.tensor_scalar(v, v, EPS, None, ALU.add).then_inc(step, 1)
                dve.wait_ge(rs_guess, guess_at)
                V.tensor_tensor(tmp, v, y, ALU.mult).then_inc(step, 1)
                dve.wait_ge(step, at + 2)
                V.tensor_tensor(tmp, tmp, y, ALU.mult).then_inc(step, 1)
                dve.wait_ge(step, at + 3)
                V.tensor_scalar(tmp, tmp, -0.5, 1.5, ALU.mult, ALU.add).then_inc(step, 1)
                dve.wait_ge(step, at + 4)
                V.tensor_tensor(y, y, tmp, ALU.mult).then_inc(step, 1)
                dve.wait_ge(step, at + 5)

            dve.wait_ge(mean_ready, 2)
            V.tensor_copy(ln["mu"], bank[2][:, 0:T]).then_inc(ln_step, 1)
            dve.wait_ge(ln_step, 3)
            V.tensor_tensor(ln["mu2"], ln["mu"], ln["mu"], ALU.mult).then_inc(ln_step, 1)
            dve.wait_ge(ln_step, 4)
            dve.wait_ge(mean_ready, 3)
            V.tensor_tensor(ln["var"], bank[3][:, 0:T], ln["mu2"], ALU.subtract).then_inc(ln_step, 1)
            dve.wait_ge(ln_step, 5)
            rstd(ln["rstd"], ln["var"], ln["mu2"], ln_step, 5, 2)
            mu2 = ln["mu"].rearrange("p (a t) -> p a t", a=1).to_broadcast([128, 2, T])
            rs2 = ln["rstd"].rearrange("p (a t) -> p a t", a=1).to_broadcast([128, 2, T])
            with dve.Fori(0, X_B) as n:
                hh = h[:, bass.ds(2 * n, 2), :]
                V.tensor_tensor(hh, hh, mu2, ALU.subtract).then_inc(ln_step, 1)
                dve.wait_ge(ln_step, 11 + n)
                V.tensor_tensor(hh, hh, rs2, ALU.mult).then_inc(normed, 1)
                dve.wait_ge(x_hi_ready, X_A + n + 1)
                V.tensor_tensor(x_lo[:, bass.ds(2 * n, 2), :], hh, x_hi[:, bass.ds(2 * n, 2), :].bitcast(f32),
                                ALU.subtract).then_inc(x_lo_ready, 1)

            with dve.Fori(0, B_ITERS) as i:
                P = P_B + 4 * i
                for p, half in ((2, 0), (2, 1), (3, 0), (3, 1), (4, 0)):
                    split_lo(P + p, half)
                parts = [(z_bank[0][:, 0:384], b["w"][:, 0, :], b["sp"][:, 0, :]),
                         (z_bank[1][:, 0:384], b["w"][:, 1, :], b["sp"][:, 1, :]),
                         (zM_bank[0:16, 0:2 * SEQ], b["wM"][0:16].rearrange("p a b -> p (a b)"),
                          b["spM"][0:16].rearrange("p a b -> p (a b)"))]
                dve.wait_ge(pt_copied, PT_A + 3 * i)
                for n, (z, w, s) in enumerate(parts):
                    dve.wait_ge(sp_ln, 3 * i + n + 1)
                    V.scalar_tensor_tensor(s, z, 0.0, w, ALU.max, ALU.add).then_inc(sp_ready, 1)
                for u in range(2):
                    dve.wait_ge(sp_hi_ready, 2 * i + u + 1)
                    V.tensor_tensor(sp_lo[:, u, :], b["sp"][:, u, :], sp_hi[:, u, :].bitcast(f32),
                                    ALU.subtract).then_inc(sp_lo_ready, 1)
                for u in range(2):
                    dve.wait_ge(tile_full[u], P + 3)
                    V.tensor_copy(b["vT"][:, u, :], acc[u][:, 0:T]).then_inc(tile_free[u], 1)
                split_lo(P + 4, 1)
                split_lo(P + 5, 0)
                for u in range(2):
                    dve.wait_ge(gateb_exp, 2 * i + u + 1)
                    V.tensor_scalar(b["gate"][:, u, :], b["gate"][:, u, :], 1.0, None, ALU.add) \
                     .then_inc(gateb_den, 1)
                    dve.wait_ge(gateb_den, 4 * i + 2 * u + 1)
                    V.reciprocal(b["gate"][:, u, :], b["gate"][:, u, :]).then_inc(gateb_den, 1)
                    dve.wait_ge(gateb_den, 4 * i + 2 * u + 2)
                    V.tensor_tensor(b["gate"][:, u, :], acc[u][:, 0:SEQ], b["gate"][:, u, :], ALU.mult) \
                     .then_inc(tile_free[u], 1)
                split_lo(P + 5, 1)
                for u in range(2):
                    dve.wait_ge(pv_done, PV_A + 2 * i + u + 1)
                    dve.wait_ge(tile_free[u], P + 4)
                    dve.wait_ge(og_lo_ready, O_A + 2 * i + u)
                    V.tensor_tensor(b["og"], o_b[u][:, 0:SEQ], b["gate"][:, u, :], ALU.mult).then_inc(o_read, 1)
                    dve.wait_ge(o_read, O_A + 2 * i + u + 1)
                    dve.wait_ge(og_hi_ready, O_A + 2 * i + u + 1)
                    V.tensor_tensor(og_lo[:, 2 * i + u, 0:SEQ], b["og"], og_hi[:, 2 * i + u, 0:SEQ].bitcast(f32),
                                    ALU.subtract).then_inc(og_lo_ready, 1)

            dve.wait_ge(r_ready, 8)

            def out_b(j, splits):
                for p in range(2):
                    P = P_OUT_B + 2 * j + p
                    for u in range(2):
                        r = f["r"][:, u, bass.ds(CW * (2 * j + p), CW)]
                        dve.wait_ge(tile_full[u], P + 1)
                        V.tensor_tensor(r, acc[u][:, 0:CW], r, ALU.add).then_inc(tile_free[u], 1)
                        dve.wait_ge(tile_free[u], P + 1)
                        V.bn_stats(bn_out[:, u, 2 * j + p, :], r).then_inc(summed, 1)
                    if splits:
                        split_lo(P + 2, 0)
                        split_lo(P + 2, 1)

            with dve.Fori(0, 3) as j:
                out_b(j, True)
            out_b(3, False)
            dve.wait_ge(summed, KT)
            dve.wait_ge(rows_loaded, 16)
            for u in range(2):
                V.bn_aggr(bn_mv[:, u, 0:2], bn_out[:, u, :, :]).then_inc(fin_step, 1)
            dve.wait_ge(fin_step, 2)
            rstd(bn_mv[:, :, 2:3], bn_mv[:, :, 1:2], bn_mv[:, :, 3:4], fin_step, 2, 4)
            n = 7
            for u in range(2):
                for c in range(2):
                    cut = slice(c * 1024, (c + 1) * 1024)
                    r = f["r"][:, u, cut]
                    V.tensor_scalar(r, r, bn_mv[:, u, 0:1], bn_mv[:, u, 2:3], ALU.subtract, ALU.mult) \
                     .then_inc(fin_step, 1)
                    dve.wait_ge(fin_step, n + 1)
                    V.tensor_tensor(r, r, f["gb"][:, 0, cut], ALU.mult).then_inc(fin_step, 1)
                    dve.wait_ge(fin_step, n + 2)
                    V.tensor_tensor(r, r, f["gb"][:, 1, cut], ALU.add).then_inc(out_ready, 1)
                    n += 2

        @block.gpsimd
        def _(pool):
            pool.wait_ge(tab_ready, 2)
            pool.dma_start(bass.AP(table, 0, [[TAB, 32], [1, TAB]]), setup["tab"][0:32, :]).then_inc(tab_stored, 16)
            pool.wait_ge(tab_stored, 16)
            def stage(i, first):
                ax = i // 4
                if first:
                    pool.wait_ge(tile_free[0], P_K + 1)
                    pool.wait_ge(tile_free[1], P_K + 1)
                else:
                    pool.wait_ge(scores_ready, 4 * i)
                pool.tensor_copy(a["k_cur"], a["kT"][:, ax, :]).then_inc(k_staged, 1)
                if not first:
                    pool.wait_ge(scores_read, 8 * i)

                def hankel(dst, at, rows, cols):
                    src = bass.AP(table, 4 * i * TAB + at, [[1, rows], [TAB, 4], [1, cols]])
                    pool.dma_start(dst, src).then_inc(bias_loaded, 16)

                bt = a["bias"]
                hankel(bt[:, :, 16:272], 0, 128, 256)
                hankel(bt[:, :, 288:416], 128, 128, 128)
                hankel(bt[:, :, 0:16], LOC, 128, 16)
                hankel(bt[:, :, 272:288], LOC + 128, 128, 16)
                hankel(bt[0:16, :, 416:432], 240, 16, 16)
                if first:
                    pool.wait_ge(v_copied, 4)
                else:
                    pool.wait_ge(pv_done, 4 * i)
                V4 = a["V"].rearrange("p a (x c) -> p a x c", c=128)
                VM4 = a["VM"].rearrange("p (x c) -> p x c", c=128)
                pool.tensor_copy(a["V_cur"], V4[:, :, ax, :]).then_inc(v_staged, 1)
                pool.tensor_copy(a["VM_cur"][0:16, :], VM4[0:16, ax, :]).then_inc(v_staged, 1)

            stage(0, True)
            with pool.Fori(1, A_ITERS) as i:
                stage(i, False)


def backwards(ap):
    (p, n), (step, count) = ap.ap
    return bass.AP(ap.tensor, ap.offset + step * (count - 1), [[p, n], [-step, count]])


def half_slot(P):
    if isinstance(P, int):
        return P % 2
    return P.guaranteed_mod_val % 2


def ln_gb_at(ln_gb, n, t):
    return ln_gb[:, n, t:t + 1] if isinstance(t, int) else ln_gb[:, n, bass.ds(t, 1)]


def t5_bucket(d):
    d = np.maximum(d, 0)
    large = 16 + (np.log(np.maximum(d, 1).astype(np.float32) / 16) / np.log(128 / 16) * 16).astype(np.int32)
    return np.where(d < 16, d, np.minimum(large, N_BUCKETS - 1))


def kernel(**inputs):
    import concourse.bacc as _bacc
    from concourse.bass_utils import run_bass_kernel_spmd as _run

    f32 = mybir.dt.float32
    x = np.asarray(inputs["x"])[0]
    meta = np.asarray(inputs["meta_tokens"])
    rel = np.asarray(inputs["rel_bias"])
    w_a = np.asarray(inputs["w_in_a"])[0]
    sinks = np.asarray(inputs["sinks_a"])[0]
    w_oa = np.asarray(inputs["w_out_a"])[0]
    w_b = np.asarray(inputs["w_in_b"])[0]
    w_ob = np.asarray(inputs["w_out_b"])[0]
    g, bb = np.asarray(inputs["ln_g"]), np.asarray(inputs["ln_b"])

    heads = [(2 * (i // 4) + b) * 8 + 2 * (i % 4) + u for i in range(8) for u in range(2) for b in range(2)]
    feats = np.concatenate([np.arange(64 * hd, 64 * hd + 64) for hd in heads])
    qa, ga = w_a[:, feats], w_a[:, 2560 + feats]
    cols = [w_a[:, 2048:2304], w_a[:, 2304:2560], qa[:, 0:CW]]
    for i in range(8):
        cols.append(ga[:, i * CW:(i + 1) * CW])
        if i < 7:
            cols.append(qa[:, (i + 1) * CW:(i + 2) * CW])
    cols += [w_oa[feats][:, i * CW:(i + 1) * CW] for i in range(8)]
    for i in range(8):
        cols += [w_b[:, n * D + i * CW:n * D + (i + 1) * CW] for n in range(4)]
    cols += [w_ob[:, i * CW:(i + 1) * CW] for i in range(8)]
    chunks = np.stack([c.reshape(2, HALF, 128, CW).transpose(0, 2, 1, 3) for c in cols]) \
               .reshape(N_CHUNKS, 128, HALF * CW)

    d_loc, d_all = 255 - np.arange(LOC), T - 1 - np.arange(T)
    dist = np.concatenate([d_loc, d_all])
    onehot = (t5_bucket(dist)[None, :] == np.arange(N_BUCKETS)[:, None]).astype(np.float32)
    tab_mask = np.zeros((32, TAB), np.float32)
    tab_mask[:, :LOC] = np.where((d_loc >= 0) & (d_loc < BLK), 0.0, NEG)[None, :]
    p, c = np.arange(128)[:, None], np.arange(128)[None, :]
    consts = np.stack([p == c, np.where(p >= c, NEG, 0.0), np.where(p >= c, -1.0, 0.0),
                       np.full((128, 128), -1.0), np.full((128, 128), 1.0 / D)], 1).astype(np.float32)

    arrays = {
        "xT": np.concatenate([meta, x], 0).T.reshape(KT, 128, T).transpose(1, 0, 2),
        "chunks": chunks,
        "rel_bias": rel[:, heads],
        "sinks": np.concatenate([np.tile(sinks[heads[4 * i:4 * i + 4]], 3) for i in range(8)])[None, :],
        "onehot": onehot,
        "tab_mask": tab_mask,
        "consts": consts,
        "ln_cols": np.stack([g[0].reshape(KT, 128).T, bb[0].reshape(KT, 128).T], 1),
        "ln_rows": np.stack([g[1], bb[1]])[None],
    }
    arrays = {k: np.ascontiguousarray(v) for k, v in arrays.items()}
    nc = _bacc.Bacc("TRN2", target_bir_lowering=False, num_devices=1)
    aps = {k: nc.dram_tensor(k, v.shape, f32, kind="ExternalInput").ap() for k, v in arrays.items()}
    table = nc.dram_tensor("bias_table", (32, TAB), f32, kind="Internal")
    out = nc.dram_tensor("out", (SEQ, D), f32, kind="ExternalOutput").ap()
    trunk(nc, aps["xT"], aps["chunks"], aps["rel_bias"], aps["sinks"], aps["onehot"], aps["tab_mask"],
          aps["consts"], aps["ln_cols"], aps["ln_rows"], table, out)
    r = _run(nc, [arrays], core_ids=[0])
    return r.results[0]["out"].reshape(1, SEQ, D)
```

```python
import numpy as np
import concourse.bass as bass
from concourse import mybir
from contextlib import ExitStack

D = 2048
META = 16
SEQ = 256
T = META + SEQ
BLK = 128
KT = D // 128
HALF = KT // 2
CW = 256
ALPHA = (2.0 * 2) ** 0.25
EPS = 1e-5
NEG = -1e30
A_HD = 64
A_SCALE = A_HD ** -0.5
B_SCALE = 128 ** -0.5
N_BUCKETS = 32
LOC = 384
TAB = LOC + T
SW = 272 + 144 + 16

P_K, P_V, P_Q0 = 0, 1, 2
A_ITERS = 8
P_OUT_A = P_Q0 + 2 * A_ITERS
P_B = P_OUT_A + D // CW
B_ITERS = 8
P_OUT_B = P_B + 4 * B_ITERS
N_PAIRS = P_OUT_B + D // CW
N_CHUNKS = 2 * N_PAIRS
RAW_SLOTS = 2
SPLIT_SLOTS = 4
WORK = 8192


def trunk(nc, xT, chunks, rel_bias, sinks, onehot, tab_mask, consts, ln_cols, ln_rows, table, out):
    f32, f32r = mybir.dt.float32, mybir.dt.float32r
    ALU, ACT, AX = mybir.AluOpType, mybir.ActivationFunctionType, mybir.AxisListType

    with ExitStack() as ctx:
        def sb(name, shape, dt=f32):
            return ctx.enter_context(nc.sbuf_tensor(name, shape, dt))

        def sem(name):
            return ctx.enter_context(nc.semaphore(name))

        raw = sb("raw", [128, RAW_SLOTS, HALF, CW])
        w_hi = sb("w_hi", [128, SPLIT_SLOTS, HALF, CW], f32r)
        w_lo = sb("w_lo", [128, SPLIT_SLOTS, HALF, CW], f32r)
        h = sb("h", [128, KT, T])
        x_hi = sb("x_hi", [128, KT, T], f32r)
        x_lo = sb("x_lo", [128, KT, T], f32r)
        og_hi = sb("og_hi", [128, KT, T], f32r)
        og_lo = sb("og_lo", [128, KT, T], f32r)
        ident = sb("ident", [128, 128])
        ident_r = sb("ident_r", [128, 128], f32r)
        causal_r = sb("causal_r", [128, 128], f32r)
        neg_upper_r = sb("neg_upper_r", [128, 128], f32r)
        neg_ones_r = sb("neg_ones_r", [128, 128], f32r)
        neg_upper_m = sb("neg_upper_m", [META, META])
        mean_w = sb("mean_w", [128, 128])
        ln_gb = sb("ln_gb", [128, 2, KT])
        neg_sink = sb("neg_sink", [128, A_ITERS * 12])
        sp_hi = sb("sp_hi", [128, 2, 384], f32r)
        sp_lo = sb("sp_lo", [128, 2, 384], f32r)
        small = sb("small", [128, 7, 12])
        row_max, neg_max, sink_exp, row_sum, denom, rinv, sink_shift = (small[:, n, :] for n in range(7))
        bn_out = sb("bn_out", [128, 2, D // CW, 6])
        bn_mv = sb("bn_mv", [128, 2, 4])

        work = sb("work", [128, WORK])

        def carve(sizes):
            at, views = 0, {}
            for name, shape in sizes:
                n = int(np.prod(shape))
                v = work[:, at:at + n]
                if len(shape) == 2:
                    v = v.rearrange("p (a b) -> p a b", b=shape[1])
                if len(shape) == 3:
                    v = v.rearrange("p (a b c) -> p a b c", b=shape[1], c=shape[2])
                views[name] = v
                at += n
            assert at <= WORK, (at, WORK)
            return views

        a = carve([("q", (2, T)), ("gate", (2, T)), ("og", (T,)), ("kT", (2, T)), ("V", (2, 256)), ("VM", (256,)),
                   ("k_cur", (T,)), ("V_cur", (2, 128)), ("VM_cur", (128,)), ("bias", (4, SW)), ("t", (4, SW)),
                   ("ptx", (2, 400)), ("pty", (512,))])
        setup = carve([("skip", (4000,)), ("onehot", (TAB,)), ("mask", (TAB,)), ("rel", (N_BUCKETS,)),
                       ("consts", (4, 128)), ("tab", (TAB,)), ("sink", (A_ITERS * 12,))])
        ln = carve([("skip", (3400,)), ("shift", (T,)), ("pair", (T,)), ("c_sum", (T,)), ("sq_sum", (T,)),
                    ("sq", (2, T)), ("mu", (T,)), ("mu2", (T,)), ("rstd", (T,)), ("var", (T,))])
        b = carve([("q", (2, SEQ)), ("kT", (2, T)), ("vT", (2, T)), ("V", (2, 256)), ("VM", (2, 128)),
                   ("w", (2, 384)), ("wM", (2, SEQ)), ("sp", (2, 384)), ("spM", (2, SEQ)),
                   ("gate", (2, SEQ)), ("og", (SEQ,))])
        f = carve([("r", (2, D)), ("gb", (2, D))])

        bank = [ctx.enter_context(nc.psum_tensor(f"bank{n}", [128, 512], f32)) for n in range(8)]
        acc = bank[0:2]
        scores = bank[2:4]
        ptx_bank, pty_bank, o_a = bank[4:6], bank[6], bank[7]
        z_bank, zM_bank, o_b = bank[2:4], bank[4], bank[5:7]

        raw_loaded = [sem(f"raw_loaded{s}") for s in range(RAW_SLOTS)]
        hi_ready, lo_ready, half_used = sem("hi_ready"), sem("lo_ready"), sem("half_used")
        tile_full = [sem("tile_full0"), sem("tile_full1")]
        tile_free = [sem("tile_free0"), sem("tile_free1")]
        x_loaded = [sem(f"x_loaded{n}") for n in range(4)]
        consts_loaded, setup_loaded, consts_ready = sem("consts_loaded"), sem("setup_loaded"), sem("consts_ready")
        banks_cleared = sem("banks_cleared")
        x_hi_ready, x_lo_ready = sem("x_hi_ready"), sem("x_lo_ready")
        tab_psum, tab_ready, tab_stored, bias_loaded = (sem("tab_psum"), sem("tab_ready"), sem("tab_stored"),
                                                        sem("bias_loaded"))
        sink_ready = sem("sink_ready")
        vt_ready, v_copied, k_staged, v_staged = sem("vt_ready"), sem("v_copied"), sem("k_staged"), sem("v_staged")
        scores_ready, scores_read, max_ready, shift_step = (sem("scores_ready"), sem("scores_read"),
                                                            sem("max_ready"), sem("shift_step"))
        probs_exp, norm_step, probs_ready = sem("probs_exp"), sem("norm_step"), sem("probs_ready")
        pt_ready, pt_copied, pv_done = sem("pt_ready"), sem("pt_copied"), sem("pv_done")
        gate_exp, o_read, og_hi_ready, og_lo_ready = (sem("gate_exp"), sem("o_read"), sem("og_hi_ready"),
                                                      sem("og_lo_ready"))
        pair_sum, mean_ready, shift_ready = sem("pair_sum"), sem("mean_ready"), sem("shift_ready")
        c_ready, c_summed, sq_ready, sq_summed = sem("c_ready"), sem("c_summed"), sem("sq_ready"), sem("sq_summed")
        ln_step, normed, affine_ready = sem("ln_step"), sem("normed"), sem("affine_ready")
        z_ready, sp_abs, sp_exp, sp_ln = sem("z_ready"), sem("sp_abs"), sem("sp_exp"), sem("sp_ln")
        sp_ready, sp_hi_ready, sp_lo_ready = sem("sp_ready"), sem("sp_hi_ready"), sem("sp_lo_ready")
        tail_ready, vtb_ready, vb_copied = sem("tail_ready"), sem("vtb_ready"), sem("vb_copied")
        gateb_exp = sem("gateb_exp")
        gate_den, gateb_den, rs_guess = sem("gate_den"), sem("gateb_den"), sem("rs_guess")
        ht_ready, r_ready, rows_loaded = sem("ht_ready"), sem("r_ready"), sem("rows_loaded")
        summed, fin_step, out_ready, stored = sem("summed"), sem("fin_step"), sem("out_ready"), sem("stored")
        centred = sem("centred")

        PT_A, PV_A, O_A = 2 * 3 * A_ITERS, 4 * A_ITERS, 2 * A_ITERS

        block = ctx.enter_context(nc.Block())

        X_GROUP_A, X_GROUP_B = 4, 2
        X_A, X_B = KT // X_GROUP_A, KT // X_GROUP_B

        @block.sync
        def _(sp):
            def load(n, slot):
                sp.dma_start(raw[:, slot, :, :].rearrange("p t c -> p (t c)"), chunks[n]) \
                  .then_inc(raw_loaded[slot], 16)

            for n in range(RAW_SLOTS):
                load(n, n)
            with sp.Fori(1, N_CHUNKS // RAW_SLOTS) as r:
                for s in range(RAW_SLOTS):
                    sp.wait_ge(lo_ready, RAW_SLOTS * (r - 1) + s + 1)
                    load(RAW_SLOTS * r + s, s)
            for j in range(2):
                for c in range(4):
                    sp.wait_ge(out_ready, 4 * j + c + 1)
                    sp.dma_start(out[j * 128:(j + 1) * 128, c * 512:(c + 1) * 512],
                                 f["r"][:, j, c * 512:(c + 1) * 512]).then_inc(stored, 16)
            sp.wait_ge(stored, 16 * 8)

        @block.tensor
        def _(pe):
            mm = nc.tensor.matmul

            def project(P, m_hi, m_lo, cols, x_from=None, between=None, token_major=False, k_outer=False):
                for half in range(2):
                    pe.wait_ge(lo_ready, 2 * P + half + 1)
                    slot = 2 * half_slot(P) + half
                    order = [(u, k) for u in range(2) for k in range(HALF)]
                    if k_outer and half == 0:
                        order.sort(key=lambda uk: uk[1])
                    for u, k in order:
                        kt = half * HALF + k
                        if kt == 0 and not (isinstance(P, int) and P == 0):
                            pe.wait_ge(tile_free[u], P)
                        if x_from and u == 0 and kt % x_from[2] == 0:
                            pe.wait_ge(x_from[0], x_from[1] + kt // x_from[2] + 1)
                        whi, wlo = w_hi[:, slot, k, :], w_lo[:, slot, k, :]
                        part = slice(u * 128, u * 128 + 128)
                        if token_major:
                            o = acc[u][:, 0:CW]
                            terms = ((m_hi[:, kt, part], whi), (m_lo[:, kt, part], whi),
                                     (m_hi[:, kt, part], wlo))
                        else:
                            o = acc[u][:, 0:cols.stop - cols.start]
                            terms = ((whi[:, part], m_hi[:, kt, cols]), (whi[:, part], m_lo[:, kt, cols]),
                                     (wlo[:, part], m_hi[:, kt, cols]))
                        for n, (l, r) in enumerate(terms):
                            last = mm(o, l, r, start=(kt == 0 and n == 0), stop=(kt == KT - 1 and n == 2))
                        if half == 0 and (u, k) == order[-1]:
                            last.then_inc(half_used, 1)
                        if kt == KT - 1:
                            last.then_inc(tile_full[u], 1)
                    if half == 0 and between:
                        between()

            ALL, SEQ_COLS = slice(0, T), slice(META, T)

            project(P_K, x_hi, x_lo, ALL, x_from=(x_lo_ready, 0, X_GROUP_A), k_outer=True)
            pe.wait_ge(setup_loaded, 16 * 6)
            mm(pty_bank[0:32, 0:LOC], setup["rel"][0:32, :], setup["onehot"][0:32, 0:LOC],
               start=True, stop=True)
            mm(o_a[0:32, 0:T], setup["rel"][0:32, :], setup["onehot"][0:32, LOC:TAB],
               start=True, stop=True).then_inc(tab_psum, 1)

            project(P_V, x_hi, x_lo, ALL)

            def values_a():
                pe.wait_ge(banks_cleared, 2)
                pe.wait_ge(consts_loaded, 16 * 3)
                for u in range(2):
                    turn_value_a(u)

            def turn_value_a(u):
                pe.wait_ge(tile_free[u], P_V + 1)
                vT = a["gate"][:, u, :]
                nc.tensor.transpose(ptx_bank[u][:, 0:128], vT[:, 16:144], ident[:])
                nc.tensor.transpose(ptx_bank[u][:, 128:256], vT[:, 144:272], ident[:])
                nc.tensor.transpose(ptx_bank[u][0:16, 256:384], vT[:, 0:16], ident[:]).then_inc(vt_ready, 1)
            project(P_Q0, x_hi, x_lo, ALL, between=values_a)

            def scores_of(i):
                for c in range(4):
                    u, base = c // 2, 64 * (c % 2)
                    if c == 0:
                        pe.wait_ge(k_staged, i + 1)
                    if c % 2 == 0:
                        pe.wait_ge(tile_free[u], P_Q0 + 1 if isinstance(i, int) and i == 0 else P_Q0 + 2 * i)
                    if c >= 2 or not (isinstance(i, int) and i == 0):
                        pe.wait_ge(scores_read, 2 * (4 * i + c - 1))
                    q, k, s = a["q"][base:base + 64, u, :], a["k_cur"][base:base + 64, :], scores[c % 2]
                    mm(s[:, 0:272], q[:, 0:128], k[:, 0:272], start=True, stop=True)
                    mm(s[:, 272:416], q[:, 128:256], k[:, 0:144], start=True, stop=True)
                    mm(s[0:16, 416:432], q[:, 256:272], k[:, 0:16], start=True, stop=True) \
                        .then_inc(scores_ready, 1)

            def turn_a(i, pair):
                n = 2 * i + pair
                for b in range(2):
                    c = 2 * pair + b
                    x, y, t = ptx_bank[b], pty_bank[0:16, 256 * b:256 * b + 256], a["t"][:, c, :]
                    pe.wait_ge(probs_ready, 3 * (4 * i + c + 1))
                    if b == 0 and not (isinstance(n, int) and n == 0):
                        pe.wait_ge(pt_copied, 3 * n)
                    nc.tensor.transpose(y[:, 0:128], t[:, 0:16], ident[:])
                    nc.tensor.transpose(y[:, 128:256], t[:, 272:288], ident[:])
                    nc.tensor.transpose(x[:, 0:128], t[:, 16:144], ident[:])
                    nc.tensor.transpose(x[:, 128:256], t[:, 288:416], ident[:])
                    nc.tensor.transpose(x[0:16, 384:400], t[0:16, 416:432], ident[0:16, 0:16])
                    nc.tensor.transpose(x[:, 256:384], t[:, 144:272], ident[:]).then_inc(pt_ready, 1)

            def value_a(i, pair):
                n = 2 * i + pair
                if pair == 0:
                    pe.wait_ge(v_staged, 2 * (i + 1))
                if not (isinstance(n, int) and n == 0):
                    pe.wait_ge(o_read, n)
                pe.wait_ge(pt_copied, 3 * (n + 1))
                for b in range(2):
                    cols = slice(64 * b, 64 * b + 64)
                    x, y, o = a["ptx"][:, b, :], a["pty"][0:16, 256 * b:256 * b + 256], o_a[cols, 0:T]
                    mm(o[:, 0:256], a["VM_cur"][0:16, cols], y, start=True, stop=False)
                    mm(o[:, 256:272], a["VM_cur"][0:16, cols], x[0:16, 384:400], start=False, stop=False)
                    mm(o[:, 0:256], a["V_cur"][:, 0, cols], x[:, 0:256], start=False, stop=False)
                    mm(o[:, 0:128], a["V_cur"][:, 1, cols], x[:, 256:384], start=False, stop=True) \
                        .then_inc(pv_done, 1)

            project(P_Q0 + 1, x_hi, x_lo, ALL, between=lambda: scores_of(0))

            def body_a(i, last):
                Pg = P_Q0 + 2 * i
                project(Pg, x_hi, x_lo, ALL, between=lambda: turn_a(i - 1, 0))
                value_a(i - 1, 0)
                turn_a(i - 1, 1)
                scores_of(i)
                project(Pg + 1, x_hi, x_lo, ALL, between=lambda: value_a(i - 1, 1))

            body_a(1, False)
            with pe.Fori(2, A_ITERS - 1) as i:
                body_a(i, False)
            body_a(A_ITERS - 1, True)

            def last_heads():
                for pair in range(2):
                    turn_a(A_ITERS - 1, pair)
                    value_a(A_ITERS - 1, pair)

            project(P_OUT_A, og_hi, og_lo, ALL, x_from=(og_lo_ready, 0, 1), between=last_heads)

            def shift_mean():
                pe.wait_ge(pair_sum, 1)
                mm(bank[2][:, 0:T], mean_w[:], ln["pair"], start=True, stop=True).then_inc(mean_ready, 1)

            project(P_OUT_A + 1, og_hi, og_lo, ALL, between=shift_mean)
            with pe.Fori(1, 4) as j:
                for p in range(2):
                    project(P_OUT_A + 2 * j + p, og_hi, og_lo, ALL)
            pe.wait_ge(c_summed, KT)
            pe.wait_ge(sq_summed, KT)
            mm(bank[2][:, 0:T], mean_w[:], ln["c_sum"], start=True, stop=True).then_inc(mean_ready, 1)
            mm(bank[3][:, 0:T], mean_w[:], ln["sq_sum"], start=True, stop=True).then_inc(mean_ready, 1)

            def scores_b(i):
                for u in range(2):
                    pe.wait_ge(tile_free[u], P_B + 4 * i + 2)
                    z, q, k = z_bank[u], b["q"][:, u, :], b["kT"][:, u, :]
                    if u == 0:
                        pe.wait_ge(pt_copied, PT_A + 3 * i)
                    mm(z[:, 0:256], k[:, 16:144], q, start=True, stop=False)
                    mm(z[:, 256:384], k[:, 144:272], q[:, 128:256], start=False, stop=False)
                    mm(z[:, 0:128], ident_r[:], causal_r[:], start=False, stop=False)
                    mm(z[:, 256:384], ident_r[:], causal_r[:], start=False, stop=True).then_inc(z_ready, 1)
                for u in range(2):
                    m = mm(zM_bank[0:16, u * SEQ:(u + 1) * SEQ], b["kT"][:, u, 0:16], b["q"][:, u, :],
                           start=(u == 0), stop=(u == 1))
                m.then_inc(z_ready, 1)

            def tails(i):
                add = dict(start=False, stop=True, skip_group_check=True)
                for u in range(2):
                    pe.wait_ge(sp_lo_ready, 2 * i + u + 1)
                    for s in (sp_hi[:, u, :], sp_lo[:, u, :]):
                        mm(z_bank[u][:, 256:384], neg_upper_r[:], s[:, 256:384], **add)
                        mm(z_bank[u][:, 0:256], neg_upper_r[:], s[:, 0:256], **add)
                        m = mm(z_bank[u][:, 128:256], neg_ones_r[:], s[:, 256:384], **add)
                    m.then_inc(tail_ready, 1)
                pe.wait_ge(sp_ready, 3 * (i + 1))
                for u in range(2):
                    zm = zM_bank[0:16, u * SEQ:(u + 1) * SEQ]
                    for s in (sp_hi[:, u, :], sp_lo[:, u, :]):
                        mm(zm, neg_ones_r[:, 0:16], s[:, 0:256], **add)
                        mm(zm[:, 128:256], neg_ones_r[:, 0:16], s[:, 256:384], **add)
                    m = mm(zm, neg_upper_m[:], b["spM"][0:16, u, :], **add)
                m.then_inc(tail_ready, 1)

            def turn_values(i):
                for u in range(2):
                    pe.wait_ge(tile_free[u], P_B + 4 * i + 3)
                    if u == 0:
                        pe.wait_ge(o_read, O_A + 2 * i)
                    v, o = b["vT"][:, u, :], o_b[u]
                    nc.tensor.transpose(o[:, 0:128], v[:, 16:144], ident[:])
                    nc.tensor.transpose(o[:, 128:256], v[:, 144:272], ident[:])
                    nc.tensor.transpose(o[0:16, 256:384], v[:, 0:16], ident[:]).then_inc(vtb_ready, 1)

            def attend_b(i):
                pe.wait_ge(pt_copied, PT_A + 3 * (i + 1))
                for u in range(2):
                    pe.wait_ge(vb_copied, 4 * i + 2 * u + 2)
                    o, w = o_b[u], b["w"][:, u, :]
                    mm(o[:, 0:256], b["VM"][0:16, u, :], b["wM"][0:16, u, :], start=True, stop=False)
                    mm(o[:, 0:256], b["V"][:, u, 0:128], w[:, 0:256], start=False, stop=False)
                    mm(o[:, 128:256], b["V"][:, u, 128:256], w[:, 256:384], start=False, stop=True) \
                        .then_inc(pv_done, 1)

            with pe.Fori(0, B_ITERS) as i:
                P = P_B + 4 * i
                project(P, x_hi, x_lo, SEQ_COLS, x_from=(x_lo_ready, X_A, X_GROUP_B), k_outer=True)
                project(P + 1, x_hi, x_lo, ALL)
                project(P + 2, x_hi, x_lo, ALL, between=lambda: scores_b(i))

                def mid():
                    tails(i)
                    turn_values(i)

                project(P + 3, x_hi, x_lo, SEQ_COLS, between=mid)
                attend_b(i)

            pe.wait_ge(o_read, O_A + 2 * B_ITERS)
            for n in range(8):
                j, tg = n // 4, n % 4
                if n >= 4:
                    pe.wait_ge(r_ready, n - 3)
                for q in range(4):
                    m = nc.tensor.transpose(bank[4 + n % 4][:, q * 128:(q + 1) * 128],
                                            h[:, 4 * tg + q, META + 128 * j:META + 128 * (j + 1)], ident[:])
                m.then_inc(ht_ready, 1)
            pe.wait_ge(og_lo_ready, O_A + KT)
            with pe.Fori(0, 4) as j:
                for p in range(2):
                    project(P_OUT_B + 2 * j + p, og_hi, og_lo, None, token_major=True)

        def wait_slot_free(eng, P, half):
            if isinstance(P, int) and P < 2:
                return
            eng.wait_ge(half_used if half == 0 else tile_full[1], P - 1)

        @block.scalar
        def _(act):
            A = nc.scalar.activation

            nc.scalar.preload_act_table_set("exp_and_others")
            for n in range(X_A):
                cut = slice(n * X_GROUP_A, (n + 1) * X_GROUP_A)
                act.dma_start(h[:, cut, :], xT[:, cut, :]).then_inc(x_loaded[n], 16)

            def split_hi(P, half):
                slot = 2 * half_slot(P) + half
                act.wait_ge(raw_loaded[half], 16 * (P + 1))
                wait_slot_free(act, P, half)
                A(w_hi[:, slot, :, :], raw[:, half, :, :], ACT.Copy).then_inc(hi_ready, 1)

            def evac(P, u, dst, cols, scale=1.0):
                act.wait_ge(tile_full[u], P + 1)
                A(dst, acc[u][:, cols], ACT.Copy, scale=scale).then_inc(tile_free[u], 1)

            def x_part(n):
                act.wait_ge(x_loaded[n], 16)
                cut = slice(n * X_GROUP_A, (n + 1) * X_GROUP_A)
                A(x_hi[:, cut, :], h[:, cut, :], ACT.Copy).then_inc(x_hi_ready, 1)

            def guess_rstd(y, v, ready, at, done):
                act.wait_ge(ready, at)
                A(y, v, ACT.Ln).then_inc(rs_guess, 1)
                act.wait_ge(rs_guess, done + 1)
                A(y, y, ACT.Exp, scale=-0.5).then_inc(rs_guess, 1)

            x_part(0)
            split_hi(0, 0)
            x_part(1)
            x_part(2)
            x_part(3)
            split_hi(0, 1)
            split_hi(1, 0)
            split_hi(1, 1)
            act.wait_ge(setup_loaded, 16 * 6)
            for n, dst in enumerate((ident_r, causal_r, neg_upper_r, neg_ones_r)):
                A(dst[:], setup["consts"][:, n, :], ACT.Copy).then_inc(consts_ready, 1)
            for u in range(2):
                evac(P_K, u, a["kT"][:, u, :], slice(0, T))
            split_hi(2, 0)
            split_hi(2, 1)
            for u in range(2):
                evac(P_V, u, a["gate"][:, u, :], slice(0, T))
            split_hi(3, 0)
            for u in range(2):
                act.wait_ge(vt_ready, u + 1)
                A(a["V"][:, :, u * 128:(u + 1) * 128],
                  ptx_bank[u][:, 0:256].rearrange("p (a b) -> p a b", b=128), ACT.Copy).then_inc(v_copied, 1)
                A(a["VM"][0:16, u * 128:(u + 1) * 128], ptx_bank[u][0:16, 256:384], ACT.Copy).then_inc(v_copied, 1)
            split_hi(3, 1)
            for u in range(2):
                evac(P_Q0, u, backwards(a["q"][:, u, :]), slice(0, T), A_SCALE)
            split_hi(4, 0)
            split_hi(4, 1)

            def exps(i):
                act.wait_ge(shift_step, 2 * (i + 1))
                for c in range(4):
                    for s, (lo, n, rows) in enumerate(((0, 272, 128), (272, 144, 128), (416, 16, 16))):
                        col = 4 * s + c
                        t = a["t"][0:rows, c, lo:lo + n]
                        A(t, t, ACT.Exp, bias=neg_max[0:rows, col:col + 1],
                          accum_out=row_sum[0:rows, col:col + 1]).then_inc(probs_exp, 1)
                A(sink_exp, sink_shift, ACT.Exp).then_inc(probs_exp, 1)

            def copies(i, pair):
                n = 2 * i + pair
                if not (isinstance(n, int) and n == 0):
                    act.wait_ge(pv_done, 2 * n)
                for b in range(2):
                    act.wait_ge(pt_ready, 2 * n + b + 1)
                    A(a["ptx"][:, b, :], ptx_bank[b][:, 0:400], ACT.Copy).then_inc(pt_copied, 1)
                A(a["pty"][0:16, :], pty_bank[0:16, :], ACT.Copy).then_inc(pt_copied, 1)

            def gate_tanh(P, i):
                for u in range(2):
                    act.wait_ge(tile_full[u], P + 1)
                    if not (isinstance(i, int) and i == 0):
                        act.wait_ge(o_read, 2 * i)
                    A(a["gate"][:, u, :], acc[u][:, 0:T], ACT.Tanh, scale=0.5).then_inc(gate_exp, 1)

            def gated_hi(i, pair):
                act.wait_ge(o_read, 2 * i + pair + 1)
                A(og_hi[:, 2 * i + pair, :], a["og"], ACT.Copy).then_inc(og_hi_ready, 1)

            exps(0)
            for u in range(2):
                evac(P_Q0 + 1, u, backwards(a["q"][:, u, :]), slice(0, T), A_SCALE)
            split_hi(5, 0)
            split_hi(5, 1)

            def body_a(i, last):
                Pg = P_Q0 + 2 * i
                split_hi(Pg + 2, 0)
                copies(i - 1, 0)
                gate_tanh(Pg, i - 1)
                gated_hi(i - 1, 0)
                split_hi(Pg + 2, 1)
                copies(i - 1, 1)
                exps(i)
                split_hi(Pg + 3, 0)
                gated_hi(i - 1, 1)
                if last:
                    gate_tanh(Pg + 1, i)
                else:
                    for u in range(2):
                        evac(Pg + 1, u, backwards(a["q"][:, u, :]), slice(0, T), A_SCALE)
                split_hi(Pg + 3, 1)

            body_a(1, False)
            with act.Fori(2, A_ITERS - 1) as i:
                body_a(i, False)
            body_a(A_ITERS - 1, True)
            for pair in range(2):
                copies(A_ITERS - 1, pair)
                gated_hi(A_ITERS - 1, pair)
            nc.scalar.preload_act_table_set("natural_log_exp_and_others")

            def out_a(P, t):
                split_hi(P + 2, 0)
                split_hi(P + 2, 1)
                for u in range(2):
                    act.wait_ge(c_ready, t + u + 1)
                    if not (isinstance(t, int) and t == 0):
                        act.wait_ge(sq_summed, t + u - 1)
                    A(ln["sq"][:, u, :], h[:, t + u, :], ACT.Square).then_inc(sq_ready, 1)

            act.wait_ge(mean_ready, 1)
            A(ln["shift"], bank[2][:, 0:T], ACT.Copy, scale=float(D // CW)).then_inc(shift_ready, 1)
            out_a(P_OUT_A, 0)
            out_a(P_OUT_A + 1, 2)
            with act.Fori(1, 4) as j:
                for p in range(2):
                    out_a(P_OUT_A + 2 * j + p, 4 * j + 2 * p)
            guess_rstd(ln["rstd"], ln["var"], ln_step, 6, 0)
            with act.Fori(0, X_B) as n:
                act.wait_ge(normed, n + 1)
                for u in range(2):
                    t = 2 * n + u
                    A(h[:, t, :], h[:, t, :], ACT.Identity, scale=ln_gb_at(ln_gb, 0, t),
                      bias=ln_gb_at(ln_gb, 1, t)).then_inc(affine_ready, 1)
                act.wait_ge(affine_ready, 2 * n + 2)
                A(x_hi[:, bass.ds(2 * n, 2), :], h[:, bass.ds(2 * n, 2), :], ACT.Copy).then_inc(x_hi_ready, 1)

            with act.Fori(0, B_ITERS) as i:
                P = P_B + 4 * i
                split_hi(P + 2, 0)
                for u in range(2):
                    evac(P, u, b["q"][:, u, :], slice(0, SEQ), B_SCALE)
                split_hi(P + 2, 1)
                split_hi(P + 3, 0)
                for u in range(2):
                    evac(P + 1, u, b["kT"][:, u, :], slice(0, T))
                split_hi(P + 3, 1)
                split_hi(P + 4, 0)
                parts = [(z_bank[0][:, 0:384], b["w"][:, 0, :]), (z_bank[1][:, 0:384], b["w"][:, 1, :]),
                         (zM_bank[0:16, 0:2 * SEQ], b["wM"][0:16].rearrange("p a b -> p (a b)"))]
                act.wait_ge(pv_done, PV_A + 2 * i)
                for n, (z, w) in enumerate(parts):
                    act.wait_ge(z_ready, 3 * i + n + 1)
                    A(w, z, ACT.Abs).then_inc(sp_abs, 1)
                for n, (z, w) in enumerate(parts):
                    act.wait_ge(sp_abs, 3 * i + n + 1)
                    A(w, w, ACT.Exp, scale=-1.0).then_inc(sp_exp, 1)
                for n, (z, w) in enumerate(parts):
                    act.wait_ge(sp_exp, 3 * i + n + 1)
                    A(w, w, ACT.Ln, bias=1.0).then_inc(sp_ln, 1)
                for u in range(2):
                    act.wait_ge(sp_ready, 3 * i + u + 1)
                    A(sp_hi[:, u, :], b["sp"][:, u, :], ACT.Copy).then_inc(sp_hi_ready, 1)
                split_hi(P + 4, 1)
                split_hi(P + 5, 0)
                for n, (z, w) in enumerate(parts):
                    act.wait_ge(tail_ready, 3 * i + n + 1)
                    A(w, z, ACT.Exp).then_inc(pt_copied, 1)
                for u in range(2):
                    act.wait_ge(vtb_ready, 2 * i + u + 1)
                    A(b["V"][:, u, :], o_b[u][:, 0:256], ACT.Copy).then_inc(vb_copied, 1)
                    A(b["VM"][0:16, u, :], o_b[u][0:16, 256:384], ACT.Copy).then_inc(vb_copied, 1)
                for u in range(2):
                    act.wait_ge(tile_full[u], P + 3 + 1)
                    A(b["gate"][:, u, :], acc[u][:, 0:SEQ], ACT.Exp, scale=-1.0).then_inc(gateb_exp, 1)
                split_hi(P + 5, 1)
                for u in range(2):
                    act.wait_ge(o_read, O_A + 2 * i + u + 1)
                    A(og_hi[:, 2 * i + u, 0:SEQ], b["og"], ACT.Copy).then_inc(og_hi_ready, 1)

            act.wait_ge(og_lo_ready, O_A + KT)
            act.dma_start(f["gb"], ln_rows.to_broadcast([128, 2, D])).then_inc(rows_loaded, 16)
            for n in range(8):
                j, tg = n // 4, n % 4
                act.wait_ge(ht_ready, n + 1)
                A(f["r"][:, j, tg * 512:(tg + 1) * 512], bank[4 + n % 4][:], ACT.Copy, scale=ALPHA) \
                    .then_inc(r_ready, 1)
            with act.Fori(0, 3) as j:
                for p in range(2):
                    split_hi(P_OUT_B + 2 + 2 * j + p, 0)
                    split_hi(P_OUT_B + 2 + 2 * j + p, 1)
            for u in range(2):
                guess_rstd(bn_mv[:, u, 2:3], bn_mv[:, u, 1:2], fin_step, 6 * u + 2, 2 * u + 2)

        @block.vector
        def _(dve):
            V = nc.vector

            def split_lo(P, half):
                slot = 2 * half_slot(P) + half
                dve.wait_ge(raw_loaded[half], 16 * (P + 1))
                dve.wait_ge(hi_ready, 2 * P + half + 1)
                V.tensor_tensor(w_lo[:, slot, :, :], raw[:, half, :, :], w_hi[:, slot, :, :].bitcast(f32),
                                ALU.subtract).then_inc(lo_ready, 1)

            def x_rest(n, cut, first):
                dve.wait_ge(x_hi_ready, first + n + 1)
                V.tensor_tensor(x_lo[:, cut, :], h[:, cut, :], x_hi[:, cut, :].bitcast(f32), ALU.subtract) \
                 .then_inc(x_lo_ready, 1)

            V.memset(small[:], 0.0).then_inc(sink_ready, 1)
            for n in range(2):
                V.memset(ptx_bank[n][:, 384:400], 0.0).then_inc(banks_cleared, 1)
            for n in range(4):
                x_rest(n, slice(4 * n, 4 * n + 4), 0)
                if n == 0:
                    split_lo(0, 0)
            for P, half in ((0, 1), (1, 0), (1, 1)):
                split_lo(P, half)
            dve.wait_ge(setup_loaded, 16 * 6)
            dve.wait_ge(tab_psum, 1)
            V.tensor_tensor(setup["tab"][0:32, 0:LOC], pty_bank[0:32, 0:LOC], setup["mask"][0:32, 0:LOC],
                            ALU.add).then_inc(tab_ready, 1)
            V.tensor_tensor(setup["tab"][0:32, LOC:TAB], o_a[0:32, 0:T], setup["mask"][0:32, LOC:TAB],
                            ALU.add).then_inc(tab_ready, 1)
            V.tensor_scalar(neg_sink[:], setup["sink"], -1.0, None, ALU.mult).then_inc(sink_ready, 1)
            for P in range(2, 5):
                split_lo(P, 0)
                split_lo(P, 1)
            dve.wait_ge(sink_ready, 2)
            dve.wait_ge(consts_ready, 4)

            BLOCKS = ((0, 272, 128), (272, 144, 128), (416, 16, 16))

            def row_maxima(i):
                dve.wait_ge(bias_loaded, 80 * (i + 1))
                if not (isinstance(i, int) and i == 0):
                    dve.wait_ge(pt_ready, 4 * i)
                for c in range(4):
                    dve.wait_ge(scores_ready, 4 * i + c + 1)
                    V.tensor_tensor(a["t"][:, c, 0:416], scores[c % 2][:, 0:416], a["bias"][:, c, 0:416],
                                    ALU.add).then_inc(scores_read, 1)
                    V.tensor_tensor(a["t"][0:16, c, 416:432], scores[c % 2][0:16, 416:432],
                                    a["bias"][0:16, c, 416:432], ALU.add).then_inc(scores_read, 1)
                dve.wait_ge(scores_read, 8 * (i + 1))
                for s, (lo, n, rows) in enumerate(BLOCKS):
                    V.reduce_max(row_max[0:rows, 4 * s:4 * s + 4], a["t"][0:rows, :, lo:lo + n], axis=AX.X) \
                     .then_inc(max_ready, 1)
                dve.wait_ge(max_ready, 3 * (i + 1))
                sink = neg_sink[:, bass.ds(12 * i, 12)]
                V.scalar_tensor_tensor(neg_max, row_max, -1.0, sink, ALU.mult, ALU.min).then_inc(shift_step, 1)
                dve.wait_ge(shift_step, 2 * i + 1)
                V.tensor_tensor(sink_shift, neg_max, sink, ALU.subtract).then_inc(shift_step, 1)

            def normalise(i):
                dve.wait_ge(probs_exp, 13 * (i + 1))
                V.tensor_tensor(denom, row_sum, sink_exp, ALU.add).then_inc(norm_step, 1)
                dve.wait_ge(norm_step, 2 * i + 1)
                V.reciprocal(rinv, denom).then_inc(norm_step, 1)
                dve.wait_ge(norm_step, 2 * i + 2)
                for c in range(4):
                    for s, (lo, n, rows) in enumerate(BLOCKS):
                        col = 4 * s + c
                        t = a["t"][0:rows, c, lo:lo + n]
                        V.tensor_scalar(t, t, rinv[0:rows, col:col + 1], None, ALU.mult).then_inc(probs_ready, 1)

            def gates(P, i):
                for u in range(2):
                    dve.wait_ge(gate_exp, 2 * i + u + 1)
                    g = a["gate"][:, u, :]
                    V.scalar_tensor_tensor(g, g, 1.0, acc[u][:, 0:T], ALU.add, ALU.mult).then_inc(tile_free[u], 1)

            def gated(P, i, pair):
                dve.wait_ge(pv_done, 4 * i + 2 * pair + 2)
                dve.wait_ge(tile_free[pair], P + 1)
                if pair or not (isinstance(i, int) and i == 0):
                    dve.wait_ge(og_lo_ready, 2 * i + pair)
                V.scalar_tensor_tensor(a["og"], backwards(o_a[:, 0:T]), 0.5, a["gate"][:, pair, :],
                                       ALU.mult, ALU.mult).then_inc(o_read, 1)

            def gated_lo(i, pair):
                t = 2 * i + pair
                dve.wait_ge(o_read, t + 1)
                dve.wait_ge(og_hi_ready, t + 1)
                V.tensor_tensor(og_lo[:, t, :], a["og"], og_hi[:, t, :].bitcast(f32),
                                ALU.subtract).then_inc(og_lo_ready, 1)

            row_maxima(0)
            normalise(0)
            split_lo(5, 0)
            split_lo(5, 1)

            def body_a(i, last):
                Pg = P_Q0 + 2 * i
                split_lo(Pg + 2, 0)
                gates(Pg, i - 1)
                gated(Pg, i - 1, 0)
                gated_lo(i - 1, 0)
                row_maxima(i)
                split_lo(Pg + 2, 1)
                gated(Pg, i - 1, 1)
                normalise(i)
                split_lo(Pg + 3, 0)
                gated_lo(i - 1, 1)
                if last:
                    gates(Pg + 1, i)
                split_lo(Pg + 3, 1)

            body_a(1, False)
            with dve.Fori(2, A_ITERS - 1) as i:
                body_a(i, False)
            body_a(A_ITERS - 1, True)
            for pair in range(2):
                gated(P_OUT_A - 1, A_ITERS - 1, pair)
                gated_lo(A_ITERS - 1, pair)

            def residual(P, u, t):
                dve.wait_ge(tile_full[u], P + 1)
                V.scalar_tensor_tensor(h[:, t, :], h[:, t, :], ALPHA, acc[u][:, 0:T], ALU.mult, ALU.add) \
                 .then_inc(tile_free[u], 1)
                dve.wait_ge(tile_free[u], P + 1)

            def shifted(t):
                V.tensor_tensor(h[:, t, :], h[:, t, :], ln["shift"], ALU.subtract).then_inc(c_ready, 1)
                dve.wait_ge(c_ready, t + 1)
                V.tensor_tensor(ln["c_sum"], ln["c_sum"], h[:, t, :], ALU.add).then_inc(c_summed, 1)
                dve.wait_ge(c_summed, t + 1)

            def squared(t, u):
                dve.wait_ge(sq_ready, t + 1)
                V.tensor_tensor(ln["sq_sum"], ln["sq_sum"], ln["sq"][:, u, :], ALU.add).then_inc(sq_summed, 1)
                dve.wait_ge(sq_summed, t + 1)

            def out_a(P, t):
                for u in range(2):
                    residual(P, u, t + u)
                    shifted(t + u)
                split_lo(P + 2, 0)
                split_lo(P + 2, 1)
                for u in range(2):
                    squared(t + u, u)

            V.memset(ln["c_sum"], 0.0).then_inc(ln_step, 1)
            V.memset(ln["sq_sum"], 0.0).then_inc(ln_step, 1)
            dve.wait_ge(ln_step, 2)
            for u in range(2):
                residual(P_OUT_A, u, u)
            V.tensor_tensor(ln["pair"], h[:, 0, :], h[:, 1, :], ALU.add).then_inc(pair_sum, 1)
            dve.wait_ge(shift_ready, 1)
            for u in range(2):
                shifted(u)
            split_lo(P_OUT_A + 2, 0)
            split_lo(P_OUT_A + 2, 1)
            for u in range(2):
                squared(u, u)
            out_a(P_OUT_A + 1, 2)
            with dve.Fori(1, 4) as j:
                for p in range(2):
                    out_a(P_OUT_A + 2 * j + p, 4 * j + 2 * p)

            def rstd(y, v, tmp, step, at, guess_at):
                V.tensor_scalar(v, v, EPS, None, ALU.add).then_inc(step, 1)
                dve.wait_ge(rs_guess, guess_at)
                V.tensor_tensor(tmp, v, y, ALU.mult).then_inc(step, 1)
                dve.wait_ge(step, at + 2)
                V.tensor_tensor(tmp, tmp, y, ALU.mult).then_inc(step, 1)
                dve.wait_ge(step, at + 3)
                V.tensor_scalar(tmp, tmp, -0.5, 1.5, ALU.mult, ALU.add).then_inc(step, 1)
                dve.wait_ge(step, at + 4)
                V.tensor_tensor(y, y, tmp, ALU.mult).then_inc(step, 1)
                dve.wait_ge(step, at + 5)

            dve.wait_ge(mean_ready, 2)
            V.tensor_copy(ln["mu"], bank[2][:, 0:T]).then_inc(ln_step, 1)
            dve.wait_ge(ln_step, 3)
            V.tensor_tensor(ln["mu2"], ln["mu"], ln["mu"], ALU.mult).then_inc(ln_step, 1)
            dve.wait_ge(ln_step, 4)
            dve.wait_ge(mean_ready, 3)
            V.tensor_tensor(ln["var"], bank[3][:, 0:T], ln["mu2"], ALU.subtract).then_inc(ln_step, 1)
            dve.wait_ge(ln_step, 5)
            rstd(ln["rstd"], ln["var"], ln["mu2"], ln_step, 5, 2)
            mu2 = ln["mu"].rearrange("p (a t) -> p a t", a=1).to_broadcast([128, 2, T])
            rs2 = ln["rstd"].rearrange("p (a t) -> p a t", a=1).to_broadcast([128, 2, T])

            def normed_group(n):
                hh = h[:, bass.ds(2 * n, 2), :]
                V.tensor_tensor(hh, hh, mu2, ALU.subtract).then_inc(ln_step, 1)
                dve.wait_ge(ln_step, 11 + n)
                V.tensor_tensor(hh, hh, rs2, ALU.mult).then_inc(normed, 1)

            def x_lo_group(n):
                dve.wait_ge(x_hi_ready, X_A + n + 1)
                V.tensor_tensor(x_lo[:, bass.ds(2 * n, 2), :], h[:, bass.ds(2 * n, 2), :],
                                x_hi[:, bass.ds(2 * n, 2), :].bitcast(f32), ALU.subtract).then_inc(x_lo_ready, 1)

            normed_group(0)
            with dve.Fori(1, X_B) as n:
                normed_group(n)
                x_lo_group(n - 1)
            x_lo_group(X_B - 1)

            with dve.Fori(0, B_ITERS) as i:
                P = P_B + 4 * i
                for p, half in ((2, 0), (2, 1), (3, 0), (3, 1), (4, 0)):
                    split_lo(P + p, half)
                parts = [(z_bank[0][:, 0:384], b["w"][:, 0, :], b["sp"][:, 0, :]),
                         (z_bank[1][:, 0:384], b["w"][:, 1, :], b["sp"][:, 1, :]),
                         (zM_bank[0:16, 0:2 * SEQ], b["wM"][0:16].rearrange("p a b -> p (a b)"),
                          b["spM"][0:16].rearrange("p a b -> p (a b)"))]
                dve.wait_ge(pt_copied, PT_A + 3 * i)
                for n, (z, w, s) in enumerate(parts):
                    dve.wait_ge(sp_ln, 3 * i + n + 1)
                    V.scalar_tensor_tensor(s, z, 0.0, w, ALU.max, ALU.add).then_inc(sp_ready, 1)
                for u in range(2):
                    dve.wait_ge(sp_hi_ready, 2 * i + u + 1)
                    V.tensor_tensor(sp_lo[:, u, :], b["sp"][:, u, :], sp_hi[:, u, :].bitcast(f32),
                                    ALU.subtract).then_inc(sp_lo_ready, 1)
                for u in range(2):
                    dve.wait_ge(tile_full[u], P + 3)
                    V.tensor_copy(b["vT"][:, u, :], acc[u][:, 0:T]).then_inc(tile_free[u], 1)
                split_lo(P + 4, 1)
                split_lo(P + 5, 0)
                for u in range(2):
                    dve.wait_ge(gateb_exp, 2 * i + u + 1)
                    V.tensor_scalar(b["gate"][:, u, :], b["gate"][:, u, :], 1.0, None, ALU.add) \
                     .then_inc(gateb_den, 1)
                    dve.wait_ge(gateb_den, 4 * i + 2 * u + 1)
                    V.reciprocal(b["gate"][:, u, :], b["gate"][:, u, :]).then_inc(gateb_den, 1)
                    dve.wait_ge(gateb_den, 4 * i + 2 * u + 2)
                    V.tensor_tensor(b["gate"][:, u, :], acc[u][:, 0:SEQ], b["gate"][:, u, :], ALU.mult) \
                     .then_inc(tile_free[u], 1)
                split_lo(P + 5, 1)
                for u in range(2):
                    dve.wait_ge(pv_done, PV_A + 2 * i + u + 1)
                    dve.wait_ge(tile_free[u], P + 4)
                    dve.wait_ge(og_lo_ready, O_A + 2 * i + u)
                    V.tensor_tensor(b["og"], o_b[u][:, 0:SEQ], b["gate"][:, u, :], ALU.mult).then_inc(o_read, 1)
                    dve.wait_ge(o_read, O_A + 2 * i + u + 1)
                    dve.wait_ge(og_hi_ready, O_A + 2 * i + u + 1)
                    V.tensor_tensor(og_lo[:, 2 * i + u, 0:SEQ], b["og"], og_hi[:, 2 * i + u, 0:SEQ].bitcast(f32),
                                    ALU.subtract).then_inc(og_lo_ready, 1)

            dve.wait_ge(r_ready, 8)

            def out_b(j, splits):
                for p in range(2):
                    P = P_OUT_B + 2 * j + p
                    for u in range(2):
                        r = f["r"][:, u, bass.ds(CW * (2 * j + p), CW)]
                        dve.wait_ge(tile_full[u], P + 1)
                        V.tensor_tensor(r, acc[u][:, 0:CW], r, ALU.add).then_inc(tile_free[u], 1)
                        dve.wait_ge(tile_free[u], P + 1)
                        V.bn_stats(bn_out[:, u, 2 * j + p, :], r).then_inc(summed, 1)
                    if splits:
                        split_lo(P + 2, 0)
                        split_lo(P + 2, 1)

            with dve.Fori(0, 3) as j:
                out_b(j, True)
            out_b(3, False)
            dve.wait_ge(rows_loaded, 16)
            for u in range(2):
                dve.wait_ge(summed, KT - 1 + u)
                V.bn_aggr(bn_mv[:, u, 0:2], bn_out[:, u, :, :]).then_inc(fin_step, 1)
                dve.wait_ge(fin_step, 6 * u + 1)
                rstd(bn_mv[:, u, 2:3], bn_mv[:, u, 1:2], bn_mv[:, u, 3:4], fin_step, 6 * u + 1, 2 * u + 4)
            for u in range(2):
                for c in range(4):
                    cut = slice(c * 512, (c + 1) * 512)
                    r = f["r"][:, u, cut]
                    V.scalar_tensor_tensor(r, r, bn_mv[:, u, 0:1], f["gb"][:, 0, cut], ALU.subtract, ALU.mult) \
                     .then_inc(centred, 1)
                    dve.wait_ge(centred, 4 * u + c + 1)
                    V.scalar_tensor_tensor(r, r, bn_mv[:, u, 2:3], f["gb"][:, 1, cut], ALU.mult, ALU.add) \
                     .then_inc(out_ready, 1)

        @block.gpsimd
        def _(pool):
            pool.dma_start(setup["rel"][0:32, :], rel_bias).then_inc(setup_loaded, 16)
            pool.dma_start(setup["onehot"][0:32, :], onehot).then_inc(setup_loaded, 16)
            pool.dma_start(setup["mask"][0:32, :], tab_mask).then_inc(setup_loaded, 16)
            pool.dma_start(setup["consts"], consts[:, 0:4, :]).then_inc(setup_loaded, 16)
            pool.dma_start(setup["sink"], sinks.to_broadcast([128, A_ITERS * 12])).then_inc(setup_loaded, 16)
            pool.dma_start(neg_upper_m[:], consts[0:META, 2, 0:META]).then_inc(setup_loaded, 16)
            pool.dma_start(ident[:], consts[:, 0, :]).then_inc(consts_loaded, 16)
            pool.dma_start(mean_w[:], consts[:, 4, :]).then_inc(consts_loaded, 16)
            pool.dma_start(ln_gb[:], ln_cols).then_inc(consts_loaded, 16)
            pool.wait_ge(tab_ready, 2)
            pool.dma_start(bass.AP(table, 0, [[TAB, 32], [1, TAB]]), setup["tab"][0:32, :]).then_inc(tab_stored, 16)
            pool.wait_ge(tab_stored, 16)
            def stage(i, first):
                ax = i // 4
                if first:
                    pool.wait_ge(tile_free[0], P_K + 1)
                    pool.wait_ge(tile_free[1], P_K + 1)
                else:
                    pool.wait_ge(scores_ready, 4 * i)
                pool.tensor_copy(a["k_cur"], a["kT"][:, ax, :]).then_inc(k_staged, 1)
                if not first:
                    pool.wait_ge(scores_read, 8 * i)

                def hankel(dst, at, rows, cols):
                    src = bass.AP(table, 4 * i * TAB + at, [[1, rows], [TAB, 4], [1, cols]])
                    pool.dma_start(dst, src).then_inc(bias_loaded, 16)

                bt = a["bias"]
                hankel(bt[:, :, 16:272], 0, 128, 256)
                hankel(bt[:, :, 288:416], 128, 128, 128)
                hankel(bt[:, :, 0:16], LOC, 128, 16)
                hankel(bt[:, :, 272:288], LOC + 128, 128, 16)
                hankel(bt[0:16, :, 416:432], 240, 16, 16)
                if first:
                    pool.wait_ge(v_copied, 4)
                else:
                    pool.wait_ge(pv_done, 4 * i)
                V4 = a["V"].rearrange("p a (x c) -> p a x c", c=128)
                VM4 = a["VM"].rearrange("p (x c) -> p x c", c=128)
                pool.tensor_copy(a["V_cur"], V4[:, :, ax, :]).then_inc(v_staged, 1)
                pool.tensor_copy(a["VM_cur"][0:16, :], VM4[0:16, ax, :]).then_inc(v_staged, 1)

            stage(0, True)
            with pool.Fori(1, A_ITERS) as i:
                stage(i, False)


def backwards(ap):
    (p, n), (step, count) = ap.ap
    return bass.AP(ap.tensor, ap.offset + step * (count - 1), [[p, n], [-step, count]])


def half_slot(P):
    if isinstance(P, int):
        return P % 2
    return P.guaranteed_mod_val % 2


def ln_gb_at(ln_gb, n, t):
    return ln_gb[:, n, t:t + 1] if isinstance(t, int) else ln_gb[:, n, bass.ds(t, 1)]


def t5_bucket(d):
    d = np.maximum(d, 0)
    large = 16 + (np.log(np.maximum(d, 1).astype(np.float32) / 16) / np.log(128 / 16) * 16).astype(np.int32)
    return np.where(d < 16, d, np.minimum(large, N_BUCKETS - 1))


def kernel(**inputs):
    import concourse.bacc as _bacc
    from concourse.bass_utils import run_bass_kernel_spmd as _run

    f32 = mybir.dt.float32
    x = np.asarray(inputs["x"])[0]
    meta = np.asarray(inputs["meta_tokens"])
    rel = np.asarray(inputs["rel_bias"])
    w_a = np.asarray(inputs["w_in_a"])[0]
    sinks = np.asarray(inputs["sinks_a"])[0]
    w_oa = np.asarray(inputs["w_out_a"])[0]
    w_b = np.asarray(inputs["w_in_b"])[0]
    w_ob = np.asarray(inputs["w_out_b"])[0]
    g, bb = np.asarray(inputs["ln_g"]), np.asarray(inputs["ln_b"])

    heads = [(2 * (i // 4) + b) * 8 + 2 * (i % 4) + u for i in range(8) for u in range(2) for b in range(2)]
    feats = np.concatenate([np.arange(64 * hd, 64 * hd + 64) for hd in heads])
    qa, ga = w_a[:, feats], w_a[:, 2560 + feats]
    cols = [w_a[:, 2048:2304], w_a[:, 2304:2560], qa[:, 0:CW], qa[:, CW:2 * CW]]
    for i in range(8):
        cols.append(ga[:, i * CW:(i + 1) * CW])
        if i < 6:
            cols.append(qa[:, (i + 2) * CW:(i + 3) * CW])
    cols += [w_oa[feats][:, i * CW:(i + 1) * CW] for i in range(8)]
    for i in range(8):
        cols += [w_b[:, n * D + i * CW:n * D + (i + 1) * CW] for n in range(4)]
    cols += [w_ob[:, i * CW:(i + 1) * CW] for i in range(8)]
    chunks = np.stack([c.reshape(2, HALF, 128, CW).transpose(0, 2, 1, 3) for c in cols]) \
               .reshape(N_CHUNKS, 128, HALF * CW)

    d_loc, d_all = 255 - np.arange(LOC), T - 1 - np.arange(T)
    dist = np.concatenate([d_loc, d_all])
    onehot = (t5_bucket(dist)[None, :] == np.arange(N_BUCKETS)[:, None]).astype(np.float32)
    tab_mask = np.zeros((32, TAB), np.float32)
    tab_mask[:, :LOC] = np.where((d_loc >= 0) & (d_loc < BLK), 0.0, NEG)[None, :]
    p, c = np.arange(128)[:, None], np.arange(128)[None, :]
    consts = np.stack([p == c, np.where(p >= c, NEG, 0.0), np.where(p >= c, -1.0, 0.0),
                       np.full((128, 128), -1.0), np.full((128, 128), 1.0 / D)], 1).astype(np.float32)

    arrays = {
        "xT": np.concatenate([meta, x], 0).T.reshape(KT, 128, T).transpose(1, 0, 2),
        "chunks": chunks,
        "rel_bias": rel[:, heads],
        "sinks": np.concatenate([np.tile(sinks[heads[4 * i:4 * i + 4]], 3) for i in range(8)])[None, :],
        "onehot": onehot,
        "tab_mask": tab_mask,
        "consts": consts,
        "ln_cols": np.stack([g[0].reshape(KT, 128).T, bb[0].reshape(KT, 128).T], 1),
        "ln_rows": np.stack([g[1], bb[1]])[None],
    }
    arrays = {k: np.ascontiguousarray(v) for k, v in arrays.items()}
    nc = _bacc.Bacc("TRN2", target_bir_lowering=False, num_devices=1)
    aps = {k: nc.dram_tensor(k, v.shape, f32, kind="ExternalInput").ap() for k, v in arrays.items()}
    table = nc.dram_tensor("bias_table", (32, TAB), f32, kind="Internal")
    out = nc.dram_tensor("out", (SEQ, D), f32, kind="ExternalOutput").ap()
    trunk(nc, aps["xT"], aps["chunks"], aps["rel_bias"], aps["sinks"], aps["onehot"], aps["tab_mask"],
          aps["consts"], aps["ln_cols"], aps["ln_rows"], table, out)
    r = _run(nc, [arrays], core_ids=[0])
    return r.results[0]["out"].reshape(1, SEQ, D)
```

```python
import numpy as np
import concourse.bass as bass
from concourse import mybir
from contextlib import ExitStack

D = 2048
META = 16
SEQ = 256
T = META + SEQ
BLK = 128
KT = D // 128
HALF = KT // 2
CW = 256
ALPHA = (2.0 * 2) ** 0.25
EPS = 1e-5
NEG = -1e30
A_HD = 64
A_SCALE = A_HD ** -0.5
B_SCALE = 128 ** -0.5
N_BUCKETS = 32
LOC = 384
TAB = LOC + T
SW = 272 + 144 + 16

P_K, P_V, P_Q0 = 0, 1, 2
A_ITERS = 8
P_OUT_A = P_Q0 + 2 * A_ITERS
P_B = P_OUT_A + D // CW
B_ITERS = 8
P_OUT_B = P_B + 4 * B_ITERS
N_PAIRS = P_OUT_B + D // CW
N_CHUNKS = 2 * N_PAIRS
RAW_SLOTS = 2
SPLIT_SLOTS = 4
WORK = 2 * 2 * D


def trunk(nc, xT, chunks, rel_bias, sinks, onehot, tab_mask, consts, ln_cols, ln_rows, table, out):
    f32, f32r = mybir.dt.float32, mybir.dt.float32r
    ALU, ACT, AX = mybir.AluOpType, mybir.ActivationFunctionType, mybir.AxisListType

    with ExitStack() as ctx:
        def sb(name, shape, dt=f32):
            return ctx.enter_context(nc.sbuf_tensor(name, shape, dt))

        def sem(name):
            return ctx.enter_context(nc.semaphore(name))

        raw = sb("raw", [128, RAW_SLOTS, HALF, CW])
        w_hi = sb("w_hi", [128, SPLIT_SLOTS, HALF, CW], f32r)
        w_lo = sb("w_lo", [128, SPLIT_SLOTS, HALF, CW], f32r)
        h = sb("h", [128, KT, T])
        x_hi = sb("x_hi", [128, KT, T], f32r)
        x_lo = sb("x_lo", [128, KT, T], f32r)
        og_hi = sb("og_hi", [128, KT, T], f32r)
        og_lo = sb("og_lo", [128, KT, T], f32r)
        ident = sb("ident", [128, 128])
        ident_r = sb("ident_r", [128, 128], f32r)
        causal_r = sb("causal_r", [128, 128], f32r)
        neg_upper_r = sb("neg_upper_r", [128, 128], f32r)
        neg_ones_r = sb("neg_ones_r", [128, 128], f32r)
        neg_ones_m = sb("neg_ones_m", [128, 128], f32r)
        neg_upper_m = sb("neg_upper_m", [64, META])
        mean_w = sb("mean_w", [128, 128])
        ln_gb = sb("ln_gb", [128, 2, KT])
        neg_sink = sb("neg_sink", [128, A_ITERS * 12])
        parts_r = sb("parts_r", [128, 4, 384], f32r)
        sp_hi, sp_lo = parts_r[:, 0:2, :], parts_r[:, 2:4, :]
        flat_r = parts_r.rearrange("p a b -> p (a b)")
        q_hi, q_lo = (flat_r[:, n * T * 2:(n + 1) * T * 2].rearrange("p (a b) -> p a b", b=T) for n in range(2))
        k_hi_cur, k_lo_cur = og_hi[:, KT - 1, :], og_lo[:, KT - 1, :]
        small = sb("small", [128, 7, 12])
        row_max, neg_max, sink_exp, row_sum, denom, rinv, sink_shift = (small[:, n, :] for n in range(7))
        bn_out = sb("bn_out", [128, 2, D // CW, 6])
        bn_mv = sb("bn_mv", [128, 2, 4])

        work = sb("work", [128, WORK])

        def carve(sizes):
            at, views = 0, {}
            for name, shape in sizes:
                n = int(np.prod(shape))
                v = work[:, at:at + n]
                if len(shape) == 2:
                    v = v.rearrange("p (a b) -> p a b", b=shape[1])
                if len(shape) == 3:
                    v = v.rearrange("p (a b c) -> p a b c", b=shape[1], c=shape[2])
                views[name] = v
                at += n
            assert at <= WORK, (at, WORK)
            return views

        a = carve([("q", (2, T)), ("gate", (2, T)), ("og", (T,)), ("kT", (2, T)), ("V", (2, 256)), ("VM", (256,)),
                   ("V_cur", (2, 128)), ("VM_cur", (128,)), ("bias", (4, SW)), ("t", (4, SW)),
                   ("ptx", (2, 400)), ("pty", (512,))])
        setup = carve([("skip", (4000,)), ("onehot", (TAB,)), ("mask", (TAB,)), ("rel", (N_BUCKETS,)),
                       ("consts", (5, 128)), ("tab", (TAB,)), ("sink", (A_ITERS * 12,))])
        ln = carve([("skip", (3400,)), ("shift", (T,)), ("pair", (T,)), ("c_sum", (T,)), ("sq_sum", (T,)),
                    ("sq", (2, T)), ("mu", (T,)), ("mu2", (T,)), ("rstd", (T,)), ("var", (T,))])
        b = carve([("q", (2, SEQ)), ("kT", (2, T)), ("vT", (2, T)), ("V", (2, 256)), ("VM", (128,)),
                   ("w", (2, 384)), ("wM", (SEQ,)), ("sp", (2, 384)), ("spM", (SEQ,)),
                   ("gate", (2, SEQ)), ("og", (SEQ,))])
        f = carve([("r", (2, D)), ("gb", (2, D))])

        bank = [ctx.enter_context(nc.psum_tensor(f"bank{n}", [128, 512], f32)) for n in range(8)]
        acc = bank[0:2]
        scores = bank[2:4]
        ptx_bank, pty_bank, o_a = bank[4:6], bank[6], bank[7]
        z_bank, zM_bank, o_b = bank[2:4], bank[4], bank[5:7]
        last_acc = (bank[2:4], bank[4:6])
        k_acc_0 = bank[5:7]

        raw_loaded = [sem(f"raw_loaded{s}") for s in range(RAW_SLOTS)]
        hi_ready, lo_ready, half_used = sem("hi_ready"), sem("lo_ready"), sem("half_used")
        tile_full = [sem("tile_full0"), sem("tile_full1")]
        tile_free = [sem("tile_free0"), sem("tile_free1")]
        x_loaded = [sem(f"x_loaded{n}") for n in range(5)]
        first_loaded = [sem(f"first_loaded{n}") for n in range(6)]
        first_hi, first_lo = sem("first_hi"), sem("first_lo")
        consts_loaded, setup_loaded, consts_ready = sem("consts_loaded"), sem("setup_loaded"), sem("consts_ready")
        banks_cleared = sem("banks_cleared")
        x_hi_ready, x_lo_ready = sem("x_hi_ready"), sem("x_lo_ready")
        tab_psum, tab_ready, tab_stored, bias_loaded = (sem("tab_psum"), sem("tab_ready"), sem("tab_stored"),
                                                        sem("bias_loaded"))
        sink_ready, q_hi_ready, q_lo_ready = sem("sink_ready"), sem("q_hi_ready"), sem("q_lo_ready")
        vt_ready, v_copied, k_staged, v_staged = sem("vt_ready"), sem("v_copied"), sem("k_staged"), sem("v_staged")
        scores_ready, scores_read, max_ready, shift_step = (sem("scores_ready"), sem("scores_read"),
                                                            sem("max_ready"), sem("shift_step"))
        probs_exp, norm_step, probs_ready = sem("probs_exp"), sem("norm_step"), sem("probs_ready")
        pt_ready, pt_copied, pv_done = sem("pt_ready"), sem("pt_copied"), sem("pv_done")
        gate_exp, o_read, og_hi_ready, og_lo_ready = (sem("gate_exp"), sem("o_read"), sem("og_hi_ready"),
                                                      sem("og_lo_ready"))
        pair_sum, mean_ready, shift_ready = sem("pair_sum"), sem("mean_ready"), sem("shift_ready")
        c_ready, c_summed, sq_ready, sq_summed = sem("c_ready"), sem("c_summed"), sem("sq_ready"), sem("sq_summed")
        ln_step, normed, h_offset = sem("ln_step"), sem("normed"), sem("h_offset")
        prepared_rows, mu_copied, rows_centred = sem("prepared_rows"), sem("mu_copied"), sem("rows_centred")
        z_ready, sp_abs, sp_exp, sp_ln = sem("z_ready"), sem("sp_abs"), sem("sp_exp"), sem("sp_ln")
        sp_ready, sp_hi_ready, sp_lo_ready = sem("sp_ready"), sem("sp_hi_ready"), sem("sp_lo_ready")
        tail_ready, vtb_ready, vb_copied = sem("tail_ready"), sem("vtb_ready"), sem("vb_copied")
        gateb_exp, gateb_den, rs_guess = sem("gateb_exp"), sem("gateb_den"), sem("rs_guess")
        ht_ready, r_ready, rows_loaded = sem("ht_ready"), sem("r_ready"), sem("rows_loaded")
        summed, fin_step, out_ready, stored = sem("summed"), sem("fin_step"), sem("out_ready"), sem("stored")
        centred, last_full, last_rows = sem("centred"), sem("last_full"), sem("last_rows")

        PT_A, PV_A, O_A = 2 * 3 * A_ITERS, 4 * A_ITERS, 2 * A_ITERS

        block = ctx.enter_context(nc.Block())

        X_PARTS = ((0, 2), (2, 4), (4, 8), (8, 12), (12, 16))
        X_A = len(X_PARTS)
        W_PARTS = ((0, 0, 2), (0, 2, 4), (0, 4, 6), (0, 6, 8), (1, 0, 4), (1, 4, 8))

        @block.sync
        def _(sp):
            def load(n, slot):
                sp.dma_start(raw[:, slot, :, :].rearrange("p t c -> p (t c)"), chunks[n]) \
                  .then_inc(raw_loaded[slot], 16)

            for n, (chunk, lo, hi) in enumerate(W_PARTS):
                loaded = first_loaded[n] if hi < HALF else raw_loaded[chunk]
                sp.dma_start(raw[:, chunk, lo:hi, :].rearrange("p t c -> p (t c)"),
                             chunks[chunk][:, lo * CW:hi * CW]).then_inc(loaded, 16)
            with sp.Fori(1, N_CHUNKS // RAW_SLOTS) as r:
                for s in range(RAW_SLOTS):
                    sp.wait_ge(lo_ready, RAW_SLOTS * (r - 1) + s + 1)
                    load(RAW_SLOTS * r + s, s)
            for j in range(2):
                for c in range(4):
                    sp.wait_ge(out_ready, 4 * j + c + 1)
                    sp.dma_start(out[j * 128:(j + 1) * 128, c * 512:(c + 1) * 512],
                                 f["r"][:, j, c * 512:(c + 1) * 512]).then_inc(stored, 16)
            sp.wait_ge(stored, 16 * 8)

        @block.tensor
        def _(pe):
            mm = nc.tensor.matmul

            def project(P, m_hi, m_lo, cols, x_from=None, between=None, token_major=False, k_outer=False,
                        late=None):
                for half in range(2):
                    first_pair = isinstance(P, int) and P == 0
                    if not first_pair:
                        pe.wait_ge(lo_ready, 2 * P + half + 1)
                    slot = 2 * half_slot(P) + half
                    order = [(u, k) for u in range(2) for k in range(HALF)]
                    if k_outer and half == 0:
                        order.sort(key=lambda uk: uk[1])
                    for u, k in order:
                        kt = half * HALF + k
                        if late and (half, u, k) == (1, 0, 4):
                            late()
                        if kt == 0 and not (isinstance(P, int) and P == 0):
                            pe.wait_ge(tile_free[u], P)
                        if x_from and u == 0 and kt in x_from[1]:
                            pe.wait_ge(x_from[0], x_from[1].index(kt) + 1)
                        if first_pair and u == 0:
                            for n, (chunk, lo, hi) in enumerate(W_PARTS):
                                if (chunk, lo) == (half, k):
                                    pe.wait_ge(*((lo_ready, chunk + 1) if hi == HALF
                                                 else (first_lo, n + 1 - chunk)))
                        whi, wlo = w_hi[:, slot, k, :], w_lo[:, slot, k, :]
                        part = slice(u * 128, u * 128 + 128)
                        if token_major:
                            o = acc[u][:, 0:CW]
                            terms = ((m_hi[:, kt, part], whi), (m_lo[:, kt, part], whi),
                                     (m_hi[:, kt, part], wlo))
                        else:
                            o = acc[u][:, 0:cols.stop - cols.start]
                            terms = ((whi[:, part], m_hi[:, kt, cols]), (whi[:, part], m_lo[:, kt, cols]),
                                     (wlo[:, part], m_hi[:, kt, cols]))
                        for n, (l, r) in enumerate(terms):
                            last = mm(o, l, r, start=(kt == 0 and n == 0), stop=(kt == KT - 1 and n == 2))
                        if half == 0 and (u, k) == order[-1]:
                            last.then_inc(half_used, 1)
                        if kt == KT - 1:
                            last.then_inc(tile_full[u], 1)
                    if half == 0 and between:
                        between()

            ALL, SEQ_COLS = slice(0, T), slice(META, T)

            project(P_K, x_hi, x_lo, ALL, x_from=(x_lo_ready, [lo for lo, _ in X_PARTS]), k_outer=True)
            pe.wait_ge(setup_loaded, 16 * 7)
            mm(pty_bank[0:32, 0:LOC], setup["rel"][0:32, :], setup["onehot"][0:32, 0:LOC],
               start=True, stop=True)
            mm(o_a[0:32, 0:T], setup["rel"][0:32, :], setup["onehot"][0:32, LOC:TAB],
               start=True, stop=True).then_inc(tab_psum, 1)

            project(P_V, x_hi, x_lo, ALL)

            def values_a():
                pe.wait_ge(banks_cleared, 2)
                pe.wait_ge(consts_loaded, 16 * 3)
                for u in range(2):
                    turn_value_a(u)

            def turn_value_a(u):
                pe.wait_ge(tile_free[u], P_V + 1)
                vT = a["gate"][:, u, :]
                nc.tensor.transpose(ptx_bank[u][:, 0:128], vT[:, 16:144], ident[:])
                nc.tensor.transpose(ptx_bank[u][:, 128:256], vT[:, 144:272], ident[:])
                nc.tensor.transpose(ptx_bank[u][0:16, 256:384], vT[:, 0:16], ident[:]).then_inc(vt_ready, 1)
            project(P_Q0, x_hi, x_lo, ALL, between=values_a)

            def scores_of(i, u):
                if u == 0:
                    pe.wait_ge(k_staged, 2 * (i + 1))
                    pe.wait_ge(q_lo_ready, i + 1)
                if u or not (isinstance(i, int) and i == 0):
                    pe.wait_ge(scores_read, 2 * (4 * i + 2 * u))
                for rows, (lo, n), q_cut in ((128, (0, 272), slice(0, 128)), (128, (272, 144), slice(128, 256)),
                                             (16, (416, 16), slice(256, 272))):
                    for step, (q, k) in enumerate(((q_hi, k_hi_cur), (q_hi, k_lo_cur), (q_lo, k_hi_cur))):
                        for h2 in range(2):
                            part = slice(64 * h2, 64 * h2 + 64)
                            m = mm(scores[h2][0:rows, lo:lo + n], q[part, u, q_cut], k[part, 0:n],
                                   start=(step == 0), stop=(step == 2))
                            if rows == 16 and step == 2:
                                m.then_inc(scores_ready, 1)

            def turn_a(i, pair):
                n = 2 * i + pair
                for b in range(2):
                    c = 2 * pair + b
                    x, y, t = ptx_bank[b], pty_bank[0:16, 256 * b:256 * b + 256], a["t"][:, c, :]
                    pe.wait_ge(probs_ready, 3 * (4 * i + c + 1))
                    if b == 0 and not (isinstance(n, int) and n == 0):
                        pe.wait_ge(pt_copied, 3 * n)
                    nc.tensor.transpose(y[:, 0:128], t[:, 0:16], ident[:])
                    nc.tensor.transpose(y[:, 128:256], t[:, 272:288], ident[:])
                    nc.tensor.transpose(x[:, 0:128], t[:, 16:144], ident[:])
                    nc.tensor.transpose(x[:, 128:256], t[:, 288:416], ident[:])
                    nc.tensor.transpose(x[0:16, 384:400], t[0:16, 416:432], ident[0:16, 0:16])
                    nc.tensor.transpose(x[:, 256:384], t[:, 144:272], ident[:]).then_inc(pt_ready, 1)

            def value_a(i, pair):
                n = 2 * i + pair
                if pair == 0:
                    pe.wait_ge(v_staged, 2 * (i + 1))
                if not (isinstance(n, int) and n == 0):
                    pe.wait_ge(o_read, n)
                pe.wait_ge(pt_copied, 3 * (n + 1))
                for step in range(4):
                    for b in range(2):
                        cols = slice(64 * b, 64 * b + 64)
                        x, y, o = a["ptx"][:, b, :], a["pty"][0:16, 256 * b:256 * b + 256], o_a[cols, 0:T]
                        lo, n, l, r = ((0, 256, a["VM_cur"][0:16, cols], y),
                                       (256, 16, a["VM_cur"][0:16, cols], x[0:16, 384:400]),
                                       (0, 256, a["V_cur"][:, 0, cols], x[:, 0:256]),
                                       (0, 128, a["V_cur"][:, 1, cols], x[:, 256:384]))[step]
                        m = mm(o[:, lo:lo + n], l, r, start=(step == 0), stop=(step == 3))
                        if step == 3:
                            m.then_inc(pv_done, 1)

            project(P_Q0 + 1, x_hi, x_lo, ALL, between=lambda: [scores_of(0, u) for u in range(2)])

            def body_a(i, last):
                Pg = P_Q0 + 2 * i
                project(Pg, x_hi, x_lo, ALL, between=lambda: turn_a(i - 1, 0))
                value_a(i - 1, 0)
                scores_of(i, 0)
                turn_a(i - 1, 1)
                scores_of(i, 1)
                project(Pg + 1, x_hi, x_lo, ALL, between=lambda: value_a(i - 1, 1))

            body_a(1, False)
            with pe.Fori(2, A_ITERS - 1) as i:
                body_a(i, False)
            body_a(A_ITERS - 1, True)

            def last_heads():
                value_a(A_ITERS - 1, 0)
                turn_a(A_ITERS - 1, 1)

            turn_a(A_ITERS - 1, 0)

            project(P_OUT_A, og_hi, og_lo, ALL, x_from=(og_lo_ready, list(range(KT))), between=last_heads,
                    late=lambda: value_a(A_ITERS - 1, 1))

            def shift_mean():
                pe.wait_ge(pair_sum, 1)
                mm(bank[2][:, 0:T], mean_w[:], ln["pair"], start=True, stop=True).then_inc(mean_ready, 1)

            project(P_OUT_A + 1, og_hi, og_lo, ALL, between=shift_mean)
            with pe.Fori(1, 3) as j:
                for p in range(2):
                    project(P_OUT_A + 2 * j + p, og_hi, og_lo, ALL)
            project(P_B - 2, og_hi, og_lo, ALL)

            def means():
                pe.wait_ge(c_summed, KT - 2)
                pe.wait_ge(sq_summed, KT - 2)
                mm(bank[2][:, 0:T], mean_w[:], ln["c_sum"], start=True, stop=False)
                mm(bank[3][:, 0:T], mean_w[:], ln["sq_sum"], start=True, stop=False)

            project(P_B - 1, og_hi, og_lo, ALL, late=means)
            for u in range(2):
                pe.wait_ge(tile_free[u], P_B)
                m = mm(bank[2][:, 0:T], mean_w[:], h[:, KT - 2 + u, :], start=False, stop=(u == 1))
            m.then_inc(mean_ready, 1)
            for u in range(2):
                pe.wait_ge(sq_ready, KT - 1 + u)
                m = mm(bank[3][:, 0:T], mean_w[:], ln["sq"][:, u, :], start=False, stop=(u == 1))
            m.then_inc(mean_ready, 1)

            def scores_b(i):
                for u in range(2):
                    pe.wait_ge(tile_free[u], P_B + 4 * i + 2)
                    z, q, k = z_bank[u], b["q"][:, u, :], b["kT"][:, u, :]
                    if u == 0:
                        pe.wait_ge(pt_copied, PT_A + 3 * i)
                    mm(z[:, 0:256], k[:, 16:144], q, start=True, stop=False)
                    mm(z[:, 256:384], k[:, 144:272], q[:, 128:256], start=False, stop=False)
                    mm(z[:, 0:128], ident_r[:], causal_r[:], start=False, stop=False)
                    mm(z[:, 256:384], ident_r[:], causal_r[:], start=False, stop=True).then_inc(z_ready, 1)
                for u in range(2):
                    m = mm(zM_bank[32 * u:32 * u + 32, 0:SEQ], b["kT"][:, u, 0:32], b["q"][:, u, :],
                           start=True, stop=True)
                m.then_inc(z_ready, 1)

            def tails(i):
                add = dict(start=False, stop=True, skip_group_check=True)
                for u in range(2):
                    pe.wait_ge(sp_lo_ready, 2 * i + u + 1)
                    for s in (sp_hi[:, u, :], sp_lo[:, u, :]):
                        mm(z_bank[u][:, 256:384], neg_upper_r[:], s[:, 256:384], **add)
                        mm(z_bank[u][:, 0:256], neg_upper_r[:], s[:, 0:256], **add)
                        m = mm(z_bank[u][:, 128:256], neg_ones_r[:], s[:, 256:384], **add)
                    m.then_inc(tail_ready, 1)
                pe.wait_ge(sp_ready, 3 * (i + 1))
                zm = [zM_bank[32 * u:32 * u + 32, 0:SEQ] for u in range(2)]
                for u in range(2):
                    ones = neg_ones_m[:, 32 * (1 - u):32 * (1 - u) + 64]
                    for s in (sp_hi[:, u, :], sp_lo[:, u, :]):
                        mm(zM_bank[0:64, 0:256], ones, s[:, 0:256], **add)
                        mm(zM_bank[0:64, 128:256], ones, s[:, 256:384], **add)
                for u in range(2):
                    m = mm(zm[u][0:16, :], neg_upper_m[32 * u:32 * u + 16, :], b["spM"][32 * u:32 * u + 16, :],
                           **add)
                m.then_inc(tail_ready, 1)

            def turn_values(i):
                for u in range(2):
                    pe.wait_ge(tile_free[u], P_B + 4 * i + 3)
                    if u == 0:
                        pe.wait_ge(o_read, O_A + 2 * i)
                    v, o = b["vT"][:, u, :], o_b[u]
                    nc.tensor.transpose(o[:, 0:128], v[:, 16:144], ident[:])
                    nc.tensor.transpose(o[:, 128:256], v[:, 144:272], ident[:])
                    nc.tensor.transpose(o[0:16, 256:384], v[:, 0:16], ident[:]).then_inc(vtb_ready, 1)

            def attend_b(i):
                pe.wait_ge(pt_copied, PT_A + 3 * (i + 1))
                pe.wait_ge(vb_copied, 4 * (i + 1))
                for u in range(2):
                    meta = slice(32 * u, 32 * u + 16)
                    mm(o_b[u][:, 0:256], b["VM"][meta, :], b["wM"][meta, :], start=True, stop=False)
                for u in range(2):
                    o, w = o_b[u], b["w"][:, u, :]
                    mm(o[:, 0:256], b["V"][:, u, 0:128], w[:, 0:256], start=False, stop=False)
                    mm(o[:, 128:256], b["V"][:, u, 128:256], w[:, 256:384], start=False, stop=True) \
                        .then_inc(pv_done, 1)

            def queries_and_keys_0():
                for half in range(2):
                    for k in range(HALF):
                        kt = half * HALF + k
                        for pair in range(2):
                            P = P_B + pair
                            slot = 2 * half_slot(P) + half
                            if k == 0:
                                pe.wait_ge(lo_ready, 2 * P + half + 1)
                            if kt == 0:
                                for u in range(2):
                                    pe.wait_ge(*((tile_free[u], P_B), (pt_copied, PT_A))[pair])
                            if pair == 0:
                                pe.wait_ge(x_lo_ready, X_A + kt + 1)
                            for u in range(2):
                                whi, wlo = (w[:, slot, k, u * 128:u * 128 + 128] for w in (w_hi, w_lo))
                                cols, banks = ((SEQ_COLS, acc), (ALL, k_acc_0))[pair]
                                o = banks[u][:, 0:cols.stop - cols.start]
                                xh, xl = x_hi[:, kt, cols], x_lo[:, kt, cols]
                                mm(o, whi, xh, start=(kt == 0), stop=False)
                                mm(o, whi, xl, start=False, stop=False)
                                last = mm(o, wlo, xh, start=False, stop=(kt == KT - 1))
                                if kt == KT - 1:
                                    last.then_inc(tile_full[u], 1)
                            if kt == HALF - 1:
                                last.then_inc(half_used, 1)

            def body_b(i):
                P = P_B + 4 * i
                if isinstance(i, int):
                    queries_and_keys_0()
                else:
                    project(P, x_hi, x_lo, SEQ_COLS)
                    project(P + 1, x_hi, x_lo, ALL)
                project(P + 2, x_hi, x_lo, ALL, between=lambda: scores_b(i))

                def mid():
                    tails(i)
                    turn_values(i)

                project(P + 3, x_hi, x_lo, SEQ_COLS, between=mid)
                attend_b(i)

            body_b(0)
            with pe.Fori(1, B_ITERS) as i:
                body_b(i)

            def residual_rows():
                pe.wait_ge(h_offset, 1)
                pe.wait_ge(o_read, O_A + KT)
                pe.wait_ge(pt_copied, PT_A + 3 * B_ITERS)
                for n in range(8):
                    j, tg = n // 4, n % 4
                    if n >= 6:
                        pe.wait_ge(r_ready, n - 5)
                    for q in range(4):
                        m = nc.tensor.transpose(bank[2 + n % 6][:, q * 128:(q + 1) * 128],
                                                h[:, 4 * tg + q, META + 128 * j:META + 128 * (j + 1)], ident[:])
                    m.then_inc(ht_ready, 1)
                pe.wait_ge(og_lo_ready, O_A + KT)

            pe.wait_ge(og_lo_ready, O_A + HALF)
            project(P_OUT_B, og_hi, og_lo, None, token_major=True, between=residual_rows)
            project(P_OUT_B + 1, og_hi, og_lo, None, token_major=True)
            with pe.Fori(1, 3) as j:
                for p in range(2):
                    project(P_OUT_B + 2 * j + p, og_hi, og_lo, None, token_major=True)
            for u in range(2):
                for P in (N_PAIRS - 2, N_PAIRS - 1):
                    for kt in range(KT):
                        if u == 0 and kt % HALF == 0:
                            pe.wait_ge(lo_ready, 2 * P + kt // HALF + 1)
                        slot, k = 2 * half_slot(P) + kt // HALF, kt % HALF
                        part = slice(u * 128, u * 128 + 128)
                        terms = ((og_hi, w_hi), (og_lo, w_hi), (og_hi, w_lo))
                        for n, (m, w) in enumerate(terms):
                            last = mm(last_acc[u][P % 2][:, 0:CW], m[:, kt, part], w[:, slot, k, :],
                                      start=(kt == 0 and n == 0), stop=(kt == KT - 1 and n == 2))
                    last.then_inc(last_full, 1)

        def wait_slot_free(eng, P, half):
            if isinstance(P, int) and P < 2:
                return
            eng.wait_ge(half_used if half == 0 else tile_full[1], P - 1)

        @block.scalar
        def _(act):
            A = nc.scalar.activation

            nc.scalar.preload_act_table_set("exp_and_others")
            for n, cut in enumerate(X_PARTS):
                act.dma_start(h[:, slice(*cut), :], xT[:, slice(*cut), :]).then_inc(x_loaded[n], 16)

            def split_hi(P, half):
                slot = 2 * half_slot(P) + half
                act.wait_ge(raw_loaded[half], 16 * (P + 1))
                wait_slot_free(act, P, half)
                A(w_hi[:, slot, :, :], raw[:, half, :, :], ACT.Copy).then_inc(hi_ready, 1)

            def evac(P, u, dst, cols, scale=1.0):
                act.wait_ge(tile_full[u], P + 1)
                A(dst, acc[u][:, cols], ACT.Copy, scale=scale).then_inc(tile_free[u], 1)

            def x_part(n):
                act.wait_ge(x_loaded[n], 16)
                cut = slice(*X_PARTS[n])
                A(x_hi[:, cut, :], h[:, cut, :], ACT.Copy).then_inc(x_hi_ready, 1)

            def guess_rstd(y, v, ready, at, done):
                act.wait_ge(ready, at)
                A(y, v, ACT.Ln).then_inc(rs_guess, 1)
                act.wait_ge(rs_guess, done + 1)
                A(y, y, ACT.Exp, scale=-0.5).then_inc(rs_guess, 1)

            def first_part_hi(n):
                chunk, lo, hi = W_PARTS[n]
                last = hi == HALF
                act.wait_ge(raw_loaded[chunk] if last else first_loaded[n], 16)
                A(w_hi[:, chunk, lo:hi, :], raw[:, chunk, lo:hi, :], ACT.Copy) \
                    .then_inc(hi_ready if last else first_hi, 1)

            for n in range(3):
                x_part(n)
                first_part_hi(n)
            first_part_hi(3)
            x_part(3)
            first_part_hi(4)
            first_part_hi(5)
            x_part(4)
            split_hi(1, 0)
            split_hi(1, 1)
            act.wait_ge(setup_loaded, 16 * 7)
            for n, dst in enumerate((ident_r, causal_r, neg_upper_r, neg_ones_r, neg_ones_m)):
                A(dst[:], setup["consts"][:, n, :], ACT.Copy).then_inc(consts_ready, 1)
            for u in range(2):
                evac(P_K, u, a["kT"][:, u, :], slice(0, T))
            split_hi(2, 0)
            split_hi(2, 1)
            for u in range(2):
                evac(P_V, u, a["gate"][:, u, :], slice(0, T))
            split_hi(3, 0)
            for u in range(2):
                act.wait_ge(vt_ready, u + 1)
                A(a["V"][:, :, u * 128:(u + 1) * 128],
                  ptx_bank[u][:, 0:256].rearrange("p (a b) -> p a b", b=128), ACT.Copy).then_inc(v_copied, 1)
                A(a["VM"][0:16, u * 128:(u + 1) * 128], ptx_bank[u][0:16, 256:384], ACT.Copy).then_inc(v_copied, 1)
            split_hi(3, 1)
            def queries(P, i):
                if not (isinstance(i, int) and i == 0):
                    act.wait_ge(q_lo_ready, i)
                for u in range(2):
                    evac(P, u, backwards(a["q"][:, u, :]), slice(0, T), A_SCALE)

            def queries_hi(i):
                act.wait_ge(tile_free[1], P_Q0 + 1 if isinstance(i, int) and i == 0 else P_Q0 + 2 * i)
                A(q_hi, a["q"], ACT.Copy).then_inc(q_hi_ready, 1)

            queries(P_Q0, 0)
            queries_hi(0)
            split_hi(4, 0)
            split_hi(4, 1)

            def exps(i, between=None):
                act.wait_ge(shift_step, 2 * (i + 1))
                for c in range(4):
                    if between and c == 1:
                        between()
                    for s, (lo, n, rows) in enumerate(((0, 272, 128), (272, 144, 128), (416, 16, 16))):
                        col = 4 * s + c
                        t = a["t"][0:rows, c, lo:lo + n]
                        A(t, t, ACT.Exp, bias=neg_max[0:rows, col:col + 1],
                          accum_out=row_sum[0:rows, col:col + 1]).then_inc(probs_exp, 1)
                A(sink_exp, sink_shift, ACT.Exp).then_inc(probs_exp, 1)

            def copies(i, pair):
                n = 2 * i + pair
                if not (isinstance(n, int) and n == 0):
                    act.wait_ge(pv_done, 2 * n)
                for b in range(2):
                    act.wait_ge(pt_ready, 2 * n + b + 1)
                    A(a["ptx"][:, b, :], ptx_bank[b][:, 0:400], ACT.Copy).then_inc(pt_copied, 1)
                A(a["pty"][0:16, :], pty_bank[0:16, :], ACT.Copy).then_inc(pt_copied, 1)

            def gate_tanh(P, i):
                for u in range(2):
                    act.wait_ge(tile_full[u], P + 1)
                    if not (isinstance(i, int) and i == 0):
                        act.wait_ge(o_read, 2 * i)
                    A(a["gate"][:, u, :], acc[u][:, 0:T], ACT.Tanh, scale=0.5).then_inc(gate_exp, 1)

            def gated_hi(i, pair):
                act.wait_ge(o_read, 2 * i + pair + 1)
                A(og_hi[:, 2 * i + pair, :], a["og"], ACT.Copy).then_inc(og_hi_ready, 1)

            split_hi(5, 0)
            exps(0, between=lambda: queries(P_Q0 + 1, 1))
            queries_hi(1)
            split_hi(5, 1)

            def body_a(i, last):
                Pg = P_Q0 + 2 * i
                split_hi(Pg + 2, 0)
                copies(i - 1, 0)
                gate_tanh(Pg, i - 1)
                gated_hi(i - 1, 0)
                split_hi(Pg + 2, 1)
                copies(i - 1, 1)
                exps(i)
                if not last:
                    split_hi(Pg + 3, 0)
                gated_hi(i - 1, 1)
                if last:
                    gate_tanh(Pg + 1, i)
                    split_hi(Pg + 3, 0)
                else:
                    queries(Pg + 1, i + 1)
                split_hi(Pg + 3, 1)
                if not last:
                    queries_hi(i + 1)

            body_a(1, False)
            with act.Fori(2, A_ITERS - 1) as i:
                body_a(i, False)
            body_a(A_ITERS - 1, True)
            for pair in range(2):
                copies(A_ITERS - 1, pair)
                gated_hi(A_ITERS - 1, pair)
            nc.scalar.preload_act_table_set("natural_log_exp_and_others")

            def square(t, u, ready, count):
                act.wait_ge(ready, count)
                if not (isinstance(t, int) and t + u < 2):
                    act.wait_ge(sq_summed, t + u - 1)
                A(ln["sq"][:, u, :], h[:, t + u, :], ACT.Square).then_inc(sq_ready, 1)

            split_hi(P_OUT_A + 2, 0)
            split_hi(P_OUT_A + 2, 1)
            act.wait_ge(mean_ready, 1)
            A(ln["shift"], bank[2][:, 0:T], ACT.Copy, scale=float(D // CW)).then_inc(shift_ready, 1)
            for u in range(2):
                square(0, u, c_ready, u + 1)
            with act.Fori(0, 3) as j:
                for p in range(2):
                    P = P_OUT_A + 1 + 2 * j + p
                    split_hi(P + 2, 0)
                    for u in range(2):
                        square(2 + 4 * j + 2 * p, u, tile_free[u], P + 1)
                    split_hi(P + 2, 1)
            split_hi(P_B + 1, 0)
            for u in range(2):
                square(KT - 2, u, tile_free[u], P_B)
            act.wait_ge(mean_ready, 2)
            A(ln["mu"], bank[2][:, 0:T], ACT.Copy).then_inc(mu_copied, 1)
            guess_rstd(ln["rstd"], ln["var"], ln_step, 4, 0)

            def rounded(n):
                for u in range(2):
                    t = 2 * n + u
                    act.wait_ge(normed, t + 1)
                    A(x_hi[:, t, :], h[:, t, :], ACT.Identity, bias=ln_gb_at(ln_gb, 1, t)).then_inc(x_hi_ready, 1)

            rounded(0)
            with act.Fori(1, 3) as n:
                rounded(n)
            split_hi(P_B + 1, 1)
            with act.Fori(3, KT // 2) as n:
                rounded(n)

            def body_b(i):
                P = P_B + 4 * i
                k_acc = k_acc_0 if isinstance(i, int) else acc
                split_hi(P + 2, 0)
                for u in range(2):
                    evac(P, u, b["q"][:, u, :], slice(0, SEQ), B_SCALE)
                if not isinstance(i, int):
                    split_hi(P + 2, 1)
                    split_hi(P + 3, 0)
                for u in range(2):
                    act.wait_ge(tile_full[u], P + 2)
                    A(b["kT"][:, u, :], k_acc[u][:, 0:T], ACT.Copy).then_inc(tile_free[u], 1)
                if isinstance(i, int):
                    split_hi(P + 2, 1)
                    split_hi(P + 3, 0)
                if not isinstance(i, int):
                    split_hi(P + 3, 1)
                    split_hi(P + 4, 0)
                parts = [(z_bank[0][:, 0:384], b["w"][:, 0, :]), (z_bank[1][:, 0:384], b["w"][:, 1, :]),
                         (zM_bank[0:64, 0:SEQ], b["wM"][0:64, :])]
                act.wait_ge(pv_done, PV_A + 2 * i)
                for n, (z, w) in enumerate(parts):
                    act.wait_ge(z_ready, 3 * i + n + 1)
                    A(w, z, ACT.Abs).then_inc(sp_abs, 1)
                for n, (z, w) in enumerate(parts):
                    act.wait_ge(sp_abs, 3 * i + n + 1)
                    A(w, w, ACT.Exp, scale=-1.0).then_inc(sp_exp, 1)
                for n, (z, w) in enumerate(parts):
                    act.wait_ge(sp_exp, 3 * i + n + 1)
                    A(w, w, ACT.Ln, bias=1.0).then_inc(sp_ln, 1)
                for u in range(2):
                    act.wait_ge(sp_ready, 3 * i + u + 1)
                    A(sp_hi[:, u, :], b["sp"][:, u, :], ACT.Copy).then_inc(sp_hi_ready, 1)
                if isinstance(i, int):
                    split_hi(P + 3, 1)
                    split_hi(P + 4, 0)
                split_hi(P + 4, 1)
                split_hi(P + 5, 0)
                for n, (z, w) in enumerate(parts):
                    act.wait_ge(tail_ready, 3 * i + n + 1)
                    A(w, z, ACT.Exp).then_inc(pt_copied, 1)
                for u in range(2):
                    act.wait_ge(vtb_ready, 2 * i + u + 1)
                    A(b["V"][:, u, :], o_b[u][:, 0:256], ACT.Copy).then_inc(vb_copied, 1)
                    A(b["VM"][32 * u:32 * u + 16, :], o_b[u][0:16, 256:384], ACT.Copy).then_inc(vb_copied, 1)
                for u in range(2):
                    act.wait_ge(tile_full[u], P + 3 + 1)
                    A(b["gate"][:, u, :], acc[u][:, 0:SEQ], ACT.Exp, scale=-1.0).then_inc(gateb_exp, 1)
                split_hi(P + 5, 1)
                for u in range(2):
                    act.wait_ge(o_read, O_A + 2 * i + u + 1)
                    A(og_hi[:, 2 * i + u, 0:SEQ], b["og"], ACT.Copy).then_inc(og_hi_ready, 1)

            body_b(0)
            with act.Fori(1, B_ITERS) as i:
                body_b(i)

            act.wait_ge(og_lo_ready, O_A + KT)
            act.dma_start(f["gb"], ln_rows.to_broadcast([128, 2, D])).then_inc(rows_loaded, 16)
            for n in range(8):
                j, tg = n // 4, n % 4
                act.wait_ge(ht_ready, n + 1)
                A(f["r"][:, j, tg * 512:(tg + 1) * 512], bank[2 + n % 6][:], ACT.Copy, scale=ALPHA) \
                    .then_inc(r_ready, 1)
            with act.Fori(0, 3) as j:
                for p in range(2):
                    split_hi(P_OUT_B + 2 + 2 * j + p, 0)
                    split_hi(P_OUT_B + 2 + 2 * j + p, 1)
            for u in range(2):
                guess_rstd(bn_mv[:, u, 2:3], bn_mv[:, u, 1:2], fin_step, 5 * u + 2, 2 * u + 2)

        @block.vector
        def _(dve):
            V = nc.vector

            def split_lo(P, half):
                slot = 2 * half_slot(P) + half
                dve.wait_ge(raw_loaded[half], 16 * (P + 1))
                dve.wait_ge(hi_ready, 2 * P + half + 1)
                V.tensor_tensor(w_lo[:, slot, :, :], raw[:, half, :, :], w_hi[:, slot, :, :].bitcast(f32),
                                ALU.subtract).then_inc(lo_ready, 1)

            def x_rest(n):
                cut = slice(*X_PARTS[n])
                dve.wait_ge(x_hi_ready, n + 1)
                V.tensor_tensor(x_lo[:, cut, :], h[:, cut, :], x_hi[:, cut, :].bitcast(f32), ALU.subtract) \
                 .then_inc(x_lo_ready, 1)

            V.memset(small[:], 0.0).then_inc(sink_ready, 1)
            for n in range(2):
                V.memset(ptx_bank[n][:, 384:400], 0.0).then_inc(banks_cleared, 1)
            def first_part_lo(n):
                chunk, lo, hi = W_PARTS[n]
                if hi == HALF:
                    dve.wait_ge(raw_loaded[chunk], 16)
                    dve.wait_ge(hi_ready, chunk + 1)
                else:
                    dve.wait_ge(first_loaded[n], 16)
                    dve.wait_ge(first_hi, n + 1 - chunk)
                V.tensor_tensor(w_lo[:, chunk, lo:hi, :], raw[:, chunk, lo:hi, :],
                                w_hi[:, chunk, lo:hi, :].bitcast(f32), ALU.subtract) \
                 .then_inc(lo_ready if hi == HALF else first_lo, 1)

            for n in range(3):
                x_rest(n)
                first_part_lo(n)
            first_part_lo(3)
            x_rest(3)
            first_part_lo(4)
            first_part_lo(5)
            x_rest(4)
            for P, half in ((1, 0), (1, 1)):
                split_lo(P, half)
            dve.wait_ge(setup_loaded, 16 * 7)
            dve.wait_ge(tab_psum, 1)
            V.tensor_tensor(setup["tab"][0:32, 0:LOC], pty_bank[0:32, 0:LOC], setup["mask"][0:32, 0:LOC],
                            ALU.add).then_inc(tab_ready, 1)
            V.tensor_tensor(setup["tab"][0:32, LOC:TAB], o_a[0:32, 0:T], setup["mask"][0:32, LOC:TAB],
                            ALU.add).then_inc(tab_ready, 1)
            V.tensor_scalar(neg_sink[:], setup["sink"], -1.0, None, ALU.mult).then_inc(sink_ready, 1)
            def queries_lo(i):
                dve.wait_ge(q_hi_ready, i + 1)
                V.tensor_tensor(q_lo, a["q"], q_hi.bitcast(f32), ALU.subtract).then_inc(q_lo_ready, 1)

            for P, half in ((2, 0), (2, 1), (3, 0), (3, 1)):
                split_lo(P, half)
            queries_lo(0)
            split_lo(4, 0)
            dve.wait_ge(sink_ready, 2)
            dve.wait_ge(consts_ready, 5)

            BLOCKS = ((0, 272, 128), (272, 144, 128), (416, 16, 16))

            def row_maxima(i):
                dve.wait_ge(bias_loaded, 80 * (i + 1))
                for c in range(4):
                    if c % 2 == 0 and not (isinstance(i, int) and i == 0):
                        dve.wait_ge(pt_ready, 4 * i - 2 + c)
                    dve.wait_ge(scores_ready, 4 * i + c + 1)
                    V.tensor_tensor(a["t"][:, c, 0:416], scores[c % 2][:, 0:416], a["bias"][:, c, 0:416],
                                    ALU.add).then_inc(scores_read, 1)
                    V.tensor_tensor(a["t"][0:16, c, 416:432], scores[c % 2][0:16, 416:432],
                                    a["bias"][0:16, c, 416:432], ALU.add).then_inc(scores_read, 1)
                dve.wait_ge(scores_read, 8 * (i + 1))
                for s, (lo, n, rows) in enumerate(BLOCKS):
                    V.reduce_max(row_max[0:rows, 4 * s:4 * s + 4], a["t"][0:rows, :, lo:lo + n], axis=AX.X) \
                     .then_inc(max_ready, 1)
                dve.wait_ge(max_ready, 3 * (i + 1))
                sink = neg_sink[:, bass.ds(12 * i, 12)]
                V.scalar_tensor_tensor(neg_max, row_max, -1.0, sink, ALU.mult, ALU.min).then_inc(shift_step, 1)
                dve.wait_ge(shift_step, 2 * i + 1)
                V.tensor_tensor(sink_shift, neg_max, sink, ALU.subtract).then_inc(shift_step, 1)

            def normalise(i):
                dve.wait_ge(probs_exp, 13 * (i + 1))
                V.tensor_tensor(denom, row_sum, sink_exp, ALU.add).then_inc(norm_step, 1)
                dve.wait_ge(norm_step, 2 * i + 1)
                V.reciprocal(rinv, denom).then_inc(norm_step, 1)
                dve.wait_ge(norm_step, 2 * i + 2)
                for c in range(4):
                    for s, (lo, n, rows) in enumerate(BLOCKS):
                        col = 4 * s + c
                        t = a["t"][0:rows, c, lo:lo + n]
                        V.tensor_scalar(t, t, rinv[0:rows, col:col + 1], None, ALU.mult).then_inc(probs_ready, 1)

            def gates(P, i):
                for u in range(2):
                    dve.wait_ge(gate_exp, 2 * i + u + 1)
                    g = a["gate"][:, u, :]
                    V.scalar_tensor_tensor(g, g, 1.0, acc[u][:, 0:T], ALU.add, ALU.mult).then_inc(tile_free[u], 1)

            def gated(P, i, pair):
                dve.wait_ge(pv_done, 4 * i + 2 * pair + 2)
                dve.wait_ge(tile_free[pair], P + 1)
                if pair or not (isinstance(i, int) and i == 0):
                    dve.wait_ge(og_lo_ready, 2 * i + pair)
                V.scalar_tensor_tensor(a["og"], backwards(o_a[:, 0:T]), 0.5, a["gate"][:, pair, :],
                                       ALU.mult, ALU.mult).then_inc(o_read, 1)

            def gated_lo(i, pair):
                t = 2 * i + pair
                dve.wait_ge(o_read, t + 1)
                dve.wait_ge(og_hi_ready, t + 1)
                V.tensor_tensor(og_lo[:, t, :], a["og"], og_hi[:, t, :].bitcast(f32),
                                ALU.subtract).then_inc(og_lo_ready, 1)

            row_maxima(0)
            split_lo(4, 1)
            split_lo(5, 0)
            normalise(0)
            queries_lo(1)
            split_lo(5, 1)

            def body_a(i, last):
                Pg = P_Q0 + 2 * i
                split_lo(Pg + 2, 0)
                gates(Pg, i - 1)
                gated(Pg, i - 1, 0)
                row_maxima(i)
                gated_lo(i - 1, 0)
                split_lo(Pg + 2, 1)
                gated(Pg, i - 1, 1)
                normalise(i)
                if last:
                    gated_lo(i - 1, 1)
                    gates(Pg + 1, i)
                    split_lo(Pg + 3, 0)
                else:
                    split_lo(Pg + 3, 0)
                    gated_lo(i - 1, 1)
                split_lo(Pg + 3, 1)
                if not last:
                    queries_lo(i + 1)

            body_a(1, False)
            with dve.Fori(2, A_ITERS - 1) as i:
                body_a(i, False)
            body_a(A_ITERS - 1, True)
            for pair in range(2):
                gated(P_OUT_A - 1, A_ITERS - 1, pair)
                gated_lo(A_ITERS - 1, pair)

            def residual(P, u, t):
                dve.wait_ge(tile_full[u], P + 1)
                V.scalar_tensor_tensor(h[:, t, :], h[:, t, :], ALPHA, acc[u][:, 0:T], ALU.mult, ALU.add) \
                 .then_inc(tile_free[u], 1)
                dve.wait_ge(tile_free[u], P + 1)

            def shifted(t):
                V.tensor_tensor(h[:, t, :], h[:, t, :], ln["shift"], ALU.subtract).then_inc(c_ready, 1)
                dve.wait_ge(c_ready, t + 1)
                V.tensor_tensor(ln["c_sum"], ln["c_sum"], h[:, t, :], ALU.add).then_inc(c_summed, 1)
                dve.wait_ge(c_summed, t + 1)

            def squared(t, u):
                dve.wait_ge(sq_ready, t + 1)
                V.tensor_tensor(ln["sq_sum"], ln["sq_sum"], ln["sq"][:, u, :], ALU.add).then_inc(sq_summed, 1)
                dve.wait_ge(sq_summed, t + 1)

            def prepared(t):
                V.scalar_tensor_tensor(h[:, t, :], h[:, t, :], ALPHA, ln["shift"], ALU.mult, ALU.subtract) \
                 .then_inc(prepared_rows, 1)

            def combined(P, u, t):
                dve.wait_ge(tile_full[u], P + 1)
                dve.wait_ge(prepared_rows, t - 1)
                V.tensor_tensor(h[:, t, :], h[:, t, :], acc[u][:, 0:T], ALU.add).then_inc(tile_free[u], 1)

            def out_a(P, t):
                for u in range(2):
                    combined(P, u, t + u)
                    if u == 0:
                        split_lo(P + 2, 0)
                    dve.wait_ge(tile_free[u], P + 1)
                    V.tensor_tensor(ln["c_sum"], ln["c_sum"], h[:, t + u, :], ALU.add).then_inc(c_summed, 1)
                    dve.wait_ge(c_summed, t + u + 1)
                    prepared(t + 2 + u)
                split_lo(P + 2, 1)
                for u in range(2):
                    squared(t + u, u)

            V.memset(ln["c_sum"], 0.0).then_inc(ln_step, 1)
            V.memset(ln["sq_sum"], 0.0).then_inc(ln_step, 1)
            dve.wait_ge(ln_step, 2)
            for u in range(2):
                residual(P_OUT_A, u, u)
            V.tensor_tensor(ln["pair"], h[:, 0, :], h[:, 1, :], ALU.add).then_inc(pair_sum, 1)
            split_lo(P_OUT_A + 2, 0)
            split_lo(P_OUT_A + 2, 1)
            dve.wait_ge(shift_ready, 1)
            for u in range(2):
                shifted(u)
            for u in range(2):
                prepared(2 + u)
            for u in range(2):
                squared(u, u)
            with dve.Fori(0, 3) as j:
                for p in range(2):
                    out_a(P_OUT_A + 1 + 2 * j + p, 2 + 4 * j + 2 * p)
            split_lo(P_B + 1, 0)
            for u in range(2):
                combined(P_B - 1, u, KT - 2 + u)

            def newton(y, v, tmp, step, at):
                V.tensor_tensor(tmp, v, y, ALU.mult).then_inc(step, 1)
                dve.wait_ge(step, at + 1)
                V.scalar_tensor_tensor(tmp, tmp, -0.5, y, ALU.mult, ALU.mult).then_inc(step, 1)
                dve.wait_ge(step, at + 2)
                V.scalar_tensor_tensor(y, tmp, 1.5, y, ALU.add, ALU.mult).then_inc(step, 1)
                dve.wait_ge(step, at + 3)

            dve.wait_ge(mu_copied, 1)
            V.tensor_tensor(ln["mu2"], ln["mu"], ln["mu"], ALU.mult).then_inc(ln_step, 1)
            dve.wait_ge(ln_step, 3)
            dve.wait_ge(mean_ready, 3)
            V.scalar_tensor_tensor(ln["var"], bank[3][:, 0:T], EPS, ln["mu2"], ALU.add, ALU.subtract) \
             .then_inc(ln_step, 1)
            mu2 = ln["mu"].rearrange("p (a t) -> p a t", a=1).to_broadcast([128, 2, T])

            def centre(n):
                hh = h[:, bass.ds(2 * n, 2), :]
                V.tensor_tensor(hh, hh, mu2, ALU.subtract).then_inc(rows_centred, 1)

            def scale_rows(n):
                dve.wait_ge(rows_centred, n + 1)
                for u in range(2):
                    t = 2 * n + u
                    V.scalar_tensor_tensor(h[:, t, :], h[:, t, :], ln_gb_at(ln_gb, 0, t), ln["rstd"],
                                           ALU.mult, ALU.mult).then_inc(normed, 1)

            def rest(n):
                for u in range(2):
                    t = 2 * n + u
                    dve.wait_ge(x_hi_ready, X_A + t + 1)
                    V.scalar_tensor_tensor(x_lo[:, t, :], h[:, t, :], ln_gb_at(ln_gb, 1, t),
                                           x_hi[:, t, :].bitcast(f32), ALU.add, ALU.subtract) \
                     .then_inc(x_lo_ready, 1)

            centre(0)
            centre(1)
            dve.wait_ge(ln_step, 4)
            dve.wait_ge(rs_guess, 2)
            newton(ln["rstd"], ln["var"], ln["mu2"], ln_step, 4)
            scale_rows(0)
            rest(0)
            with dve.Fori(1, 4) as n:
                scale_rows(n)
                centre(n + 1)
                rest(n)
            split_lo(P_B + 1, 1)
            with dve.Fori(4, KT // 2 - 1) as n:
                scale_rows(n)
                centre(n + 1)
                rest(n)
            scale_rows(KT // 2 - 1)
            rest(KT // 2 - 1)

            def body_b(i):
                P = P_B + 4 * i
                ahead = ((3, 1), (4, 0))
                for p, half in ((2, 0), (2, 1), (3, 0)) + (() if isinstance(i, int) else ahead):
                    split_lo(P + p, half)
                parts = [(z_bank[0][:, 0:384], b["w"][:, 0, :], b["sp"][:, 0, :]),
                         (z_bank[1][:, 0:384], b["w"][:, 1, :], b["sp"][:, 1, :]),
                         (zM_bank[0:64, 0:SEQ], b["wM"][0:64, :], b["spM"][0:64, :])]
                dve.wait_ge(pt_copied, PT_A + 3 * i)
                for n, (z, w, s) in enumerate(parts):
                    dve.wait_ge(sp_ln, 3 * i + n + 1)
                    V.scalar_tensor_tensor(s, z, 0.0, w, ALU.max, ALU.add).then_inc(sp_ready, 1)
                for u in range(2):
                    dve.wait_ge(sp_hi_ready, 2 * i + u + 1)
                    V.tensor_tensor(sp_lo[:, u, :], b["sp"][:, u, :], sp_hi[:, u, :].bitcast(f32),
                                    ALU.subtract).then_inc(sp_lo_ready, 1)
                for u in range(2):
                    dve.wait_ge(tile_full[u], P + 3)
                    V.tensor_copy(b["vT"][:, u, :], acc[u][:, 0:T]).then_inc(tile_free[u], 1)
                if isinstance(i, int):
                    for p, half in ahead:
                        split_lo(P + p, half)
                split_lo(P + 4, 1)
                split_lo(P + 5, 0)
                for u in range(2):
                    dve.wait_ge(gateb_exp, 2 * i + u + 1)
                    V.tensor_scalar(b["gate"][:, u, :], b["gate"][:, u, :], 1.0, None, ALU.add) \
                     .then_inc(gateb_den, 1)
                    dve.wait_ge(gateb_den, 4 * i + 2 * u + 1)
                    V.reciprocal(b["gate"][:, u, :], b["gate"][:, u, :]).then_inc(gateb_den, 1)
                    dve.wait_ge(gateb_den, 4 * i + 2 * u + 2)
                    V.tensor_tensor(b["gate"][:, u, :], acc[u][:, 0:SEQ], b["gate"][:, u, :], ALU.mult) \
                     .then_inc(tile_free[u], 1)
                split_lo(P + 5, 1)
                for u in range(2):
                    dve.wait_ge(pv_done, PV_A + 2 * i + u + 1)
                    dve.wait_ge(tile_free[u], P + 4)
                    dve.wait_ge(og_lo_ready, O_A + 2 * i + u)
                    V.tensor_tensor(b["og"], o_b[u][:, 0:SEQ], b["gate"][:, u, :], ALU.mult).then_inc(o_read, 1)
                    dve.wait_ge(o_read, O_A + 2 * i + u + 1)
                    dve.wait_ge(og_hi_ready, O_A + 2 * i + u + 1)
                    V.tensor_tensor(og_lo[:, 2 * i + u, 0:SEQ], b["og"], og_hi[:, 2 * i + u, 0:SEQ].bitcast(f32),
                                    ALU.subtract).then_inc(og_lo_ready, 1)

            body_b(0)
            with dve.Fori(1, B_ITERS) as i:
                body_b(i)

            dve.wait_ge(r_ready, 8)

            def out_cols(u, P):
                r = f["r"][:, u, bass.ds(CW * (P - P_OUT_B), CW)]
                dve.wait_ge(tile_full[u], P + 1)
                V.tensor_tensor(r, acc[u][:, 0:CW], r, ALU.add).then_inc(tile_free[u], 1)
                dve.wait_ge(tile_free[u], P + 1)
                V.bn_stats(bn_out[:, u, P - P_OUT_B, :], r).then_inc(summed, 1)

            with dve.Fori(0, 3) as j:
                for p in range(2):
                    P = P_OUT_B + 2 * j + p
                    for u in range(2):
                        out_cols(u, P)
                    split_lo(P + 2, 0)
                    split_lo(P + 2, 1)

            def last_cols(u):
                for n, P in enumerate((N_PAIRS - 2, N_PAIRS - 1)):
                    r = f["r"][:, u, CW * (P - P_OUT_B):CW * (P - P_OUT_B + 1)]
                    dve.wait_ge(last_full, 2 * u + n + 1)
                    V.tensor_tensor(r, last_acc[u][P % 2][:, 0:CW], r, ALU.add).then_inc(last_rows, 1)
                    dve.wait_ge(last_rows, 2 * u + n + 1)
                    V.bn_stats(bn_out[:, u, P - P_OUT_B, :], r).then_inc(summed, 1)

            def token_rstd(u):
                mean, var, y, tmp = (bn_mv[:, u, n:n + 1] for n in range(4))
                dve.wait_ge(summed, KT - 2 + 2 * u)
                V.bn_aggr(bn_mv[:, u, 0:2], bn_out[:, u, :, :]).then_inc(fin_step, 1)
                dve.wait_ge(fin_step, 5 * u + 1)
                V.tensor_scalar(var, var, EPS, None, ALU.add).then_inc(fin_step, 1)

            def token_newton(u):
                mean, var, y, tmp = (bn_mv[:, u, n:n + 1] for n in range(4))
                dve.wait_ge(rs_guess, 2 * u + 4)
                newton(y, var, tmp, fin_step, 5 * u + 2)

            def normalise_tokens(u, cs):
                def step(c, second):
                    cut = slice(c * 512, (c + 1) * 512)
                    r = f["r"][:, u, cut]
                    if not second:
                        V.scalar_tensor_tensor(r, r, bn_mv[:, u, 0:1], f["gb"][:, 0, cut],
                                               ALU.subtract, ALU.mult).then_inc(centred, 1)
                    else:
                        dve.wait_ge(centred, 4 * u + c + 1)
                        V.scalar_tensor_tensor(r, r, bn_mv[:, u, 2:3], f["gb"][:, 1, cut],
                                               ALU.mult, ALU.add).then_inc(out_ready, 1)

                for c in cs:
                    step(c, False)
                    if c > cs[0]:
                        step(c - 1, True)
                step(cs[-1], True)

            dve.wait_ge(rows_loaded, 16)
            last_cols(0)
            token_rstd(0)
            token_newton(0)
            normalise_tokens(0, range(4))
            last_cols(1)
            token_rstd(1)
            token_newton(1)
            normalise_tokens(1, range(4))

        @block.gpsimd
        def _(pool):
            pool.dma_start(setup["rel"][0:32, :], rel_bias).then_inc(setup_loaded, 16)
            pool.dma_start(setup["onehot"][0:32, :], onehot).then_inc(setup_loaded, 16)
            pool.dma_start(setup["mask"][0:32, :], tab_mask).then_inc(setup_loaded, 16)
            pool.dma_start(setup["consts"], consts[:, 0:5, :]).then_inc(setup_loaded, 16)
            pool.dma_start(setup["sink"], sinks.to_broadcast([128, A_ITERS * 12])).then_inc(setup_loaded, 16)
            for u in range(2):
                pool.dma_start(neg_upper_m[32 * u:32 * u + META, :], consts[0:META, 2, 0:META]) \
                    .then_inc(setup_loaded, 16)
            pool.dma_start(ident[:], consts[:, 0, :]).then_inc(consts_loaded, 16)
            pool.dma_start(mean_w[:], consts[:, 5, :]).then_inc(consts_loaded, 16)
            pool.dma_start(ln_gb[:], ln_cols).then_inc(consts_loaded, 16)
            pool.wait_ge(tab_ready, 2)
            pool.dma_start(bass.AP(table, 0, [[TAB, 32], [1, TAB]]), setup["tab"][0:32, :]).then_inc(tab_stored, 16)
            pool.wait_ge(tab_stored, 16)
            def stage(i, first):
                ax = i // 4
                if first:
                    pool.wait_ge(tile_free[0], P_K + 1)
                    pool.wait_ge(tile_free[1], P_K + 1)
                else:
                    pool.wait_ge(scores_ready, 4 * i)
                pool.tensor_copy(k_hi_cur, a["kT"][:, ax, :]).then_inc(k_staged, 1)
                pool.wait_ge(k_staged, 2 * i + 1)
                if not first:
                    pool.wait_ge(scores_read, 8 * i)

                def hankel(dst, at, rows, cols):
                    src = bass.AP(table, 4 * i * TAB + at, [[1, rows], [TAB, 4], [1, cols]])
                    pool.dma_start(dst, src).then_inc(bias_loaded, 16)

                bt = a["bias"]
                hankel(bt[:, :, 16:272], 0, 128, 256)
                hankel(bt[:, :, 288:416], 128, 128, 128)
                hankel(bt[:, :, 0:16], LOC, 128, 16)
                hankel(bt[:, :, 272:288], LOC + 128, 128, 16)
                hankel(bt[0:16, :, 416:432], 240, 16, 16)
                pool.tensor_tensor(k_lo_cur, a["kT"][:, ax, :], k_hi_cur.bitcast(f32), ALU.subtract) \
                    .then_inc(k_staged, 1)
                if first:
                    pool.wait_ge(v_copied, 4)
                else:
                    pool.wait_ge(pv_done, 4 * i)
                V4 = a["V"].rearrange("p a (x c) -> p a x c", c=128)
                VM4 = a["VM"].rearrange("p (x c) -> p x c", c=128)
                pool.tensor_copy(a["V_cur"], V4[:, :, ax, :]).then_inc(v_staged, 1)
                pool.tensor_copy(a["VM_cur"][0:16, :], VM4[0:16, ax, :]).then_inc(v_staged, 1)

            stage(0, True)
            with pool.Fori(1, A_ITERS) as i:
                stage(i, False)

            pool.wait_ge(x_lo_ready, X_A + KT)
            offset = ln_gb[:, 1, :].rearrange("p (t a) -> p t a", a=1).to_broadcast([128, KT, T])
            pool.tensor_tensor(h[:], h[:], offset, ALU.add).then_inc(h_offset, 1)


def backwards(ap):
    (p, n), (step, count) = ap.ap
    return bass.AP(ap.tensor, ap.offset + step * (count - 1), [[p, n], [-step, count]])


def half_slot(P):
    if isinstance(P, int):
        return P % 2
    return P.guaranteed_mod_val % 2


def ln_gb_at(ln_gb, n, t):
    return ln_gb[:, n, t:t + 1] if isinstance(t, int) else ln_gb[:, n, bass.ds(t, 1)]


def t5_bucket(d):
    d = np.maximum(d, 0)
    large = 16 + (np.log(np.maximum(d, 1).astype(np.float32) / 16) / np.log(128 / 16) * 16).astype(np.int32)
    return np.where(d < 16, d, np.minimum(large, N_BUCKETS - 1))


def kernel(**inputs):
    import concourse.bacc as _bacc
    from concourse.bass_utils import run_bass_kernel_spmd as _run

    f32 = mybir.dt.float32
    x = np.asarray(inputs["x"])[0]
    meta = np.asarray(inputs["meta_tokens"])
    rel = np.asarray(inputs["rel_bias"])
    w_a = np.asarray(inputs["w_in_a"])[0]
    sinks = np.asarray(inputs["sinks_a"])[0]
    w_oa = np.asarray(inputs["w_out_a"])[0]
    w_b = np.asarray(inputs["w_in_b"])[0]
    w_ob = np.asarray(inputs["w_out_b"])[0]
    g, bb = np.asarray(inputs["ln_g"]), np.asarray(inputs["ln_b"])

    heads = [(2 * (i // 4) + b) * 8 + 2 * (i % 4) + u for i in range(8) for u in range(2) for b in range(2)]
    feats = np.concatenate([np.arange(64 * hd, 64 * hd + 64) for hd in heads])
    qa, ga = w_a[:, feats], w_a[:, 2560 + feats]
    cols = [w_a[:, 2048:2304], w_a[:, 2304:2560], qa[:, 0:CW], qa[:, CW:2 * CW]]
    for i in range(8):
        cols.append(ga[:, i * CW:(i + 1) * CW])
        if i < 6:
            cols.append(qa[:, (i + 2) * CW:(i + 3) * CW])
    cols += [w_oa[feats][:, i * CW:(i + 1) * CW] for i in range(8)]
    for i in range(8):
        cols += [w_b[:, n * D + i * CW:n * D + (i + 1) * CW] for n in range(4)]
    cols += [w_ob[:, i * CW:(i + 1) * CW] for i in range(8)]
    chunks = np.stack([c.reshape(2, HALF, 128, CW).transpose(0, 2, 1, 3) for c in cols]) \
               .reshape(N_CHUNKS, 128, HALF * CW)

    d_loc, d_all = 255 - np.arange(LOC), T - 1 - np.arange(T)
    dist = np.concatenate([d_loc, d_all])
    onehot = (t5_bucket(dist)[None, :] == np.arange(N_BUCKETS)[:, None]).astype(np.float32)
    tab_mask = np.zeros((32, TAB), np.float32)
    tab_mask[:, :LOC] = np.where((d_loc >= 0) & (d_loc < BLK), 0.0, NEG)[None, :]
    p, c = np.arange(128)[:, None], np.arange(128)[None, :]
    consts = np.stack([p == c, np.where(p >= c, NEG, 0.0), np.where(p >= c, -1.0, 0.0),
                       np.full((128, 128), -1.0), np.where((c >= 32) & (c < 64) & (p >= 0), -1.0, 0.0),
                       np.full((128, 128), 1.0 / D)], 1).astype(np.float32)

    arrays = {
        "xT": np.concatenate([meta, x], 0).T.reshape(KT, 128, T).transpose(1, 0, 2),
        "chunks": chunks,
        "rel_bias": rel[:, heads],
        "sinks": np.concatenate([np.tile(sinks[heads[4 * i:4 * i + 4]], 3) for i in range(8)])[None, :],
        "onehot": onehot,
        "tab_mask": tab_mask,
        "consts": consts,
        "ln_cols": np.stack([g[0].reshape(KT, 128).T, bb[0].reshape(KT, 128).T], 1),
        "ln_rows": np.stack([g[1], bb[1]])[None],
    }
    arrays = {k: np.ascontiguousarray(v) for k, v in arrays.items()}
    nc = _bacc.Bacc("TRN2", target_bir_lowering=False, num_devices=1)
    aps = {k: nc.dram_tensor(k, v.shape, f32, kind="ExternalInput").ap() for k, v in arrays.items()}
    table = nc.dram_tensor("bias_table", (32, TAB), f32, kind="Internal")
    out = nc.dram_tensor("out", (SEQ, D), f32, kind="ExternalOutput").ap()
    trunk(nc, aps["xT"], aps["chunks"], aps["rel_bias"], aps["sinks"], aps["onehot"], aps["tab_mask"],
          aps["consts"], aps["ln_cols"], aps["ln_rows"], table, out)
    r = _run(nc, [arrays], core_ids=[0])
    return r.results[0]["out"].reshape(1, SEQ, D)
```
